# Optimizing a Trainium2 kernel written in Bass

```python
import jax, jax.numpy as jnp
from jax import lax
import numpy as np

D_MODEL = 1024
BATCH = 1
SEQ = 128
DEPTH = 1
DEC_BATCH = 1
DEC_SEQ = 256
PAST_LEN = 128

GRID_W = 64
D_A = 256
D_B = 256
D_C = 512
D_MIX = D_A + D_B + D_C
N_HEADS_C = 4
HEAD_K = D_C // N_HEADS_C
HEAD_V = D_C // N_HEADS_C
CONV_A = 3
CONV_B = 31
CHUNK = 32
N_EXPERTS = 16
N_GROUPS = 4
EXPERTS_PER_GROUP = N_EXPERTS // N_GROUPS
TOP_K = 2
GROUP_SCORE_K = 2
D_EXPERT = 512
N_MOD = 6
EPS = 1e-6
MASK_VALUE = -1e9
IN_WIDTHS = (D_A, D_A, D_A, D_B, D_B, D_C, D_C, D_C, D_C, D_C)
D_IN = sum(IN_WIDTHS)

kernel_name = 'hybrid_conv_hgrn2_moe_prefix_flow_step'

def rms_norm(x, g):
    xf = x.astype(jnp.float32)
    y = xf * lax.rsqrt(jnp.mean(xf * xf, axis=-1, keepdims=True) + EPS)
    return (y * g.astype(jnp.float32)).astype(x.dtype)

def layer_norm(x, g, b):
    xf = x.astype(jnp.float32)
    mu = jnp.mean(xf, axis=-1, keepdims=True)
    var = jnp.mean(jnp.square(xf - mu), axis=-1, keepdims=True)
    y = (xf - mu) * lax.rsqrt(var + EPS)
    return (y * g.astype(jnp.float32) + b.astype(jnp.float32)).astype(x.dtype)

def depthwise_conv(x, w):
    k = w.shape[0]
    return lax.conv_general_dilated(
        x, w[:, None, :].astype(x.dtype), window_strides=(1,), padding=[(k // 2, k // 2)],
        dimension_numbers=('NWC', 'WIO', 'NWC'), feature_group_count=x.shape[-1])

def conv_rows(x, w, layout):
    if layout == 'context':
        return depthwise_conv(x, w)
    b, t, c = x.shape
    rows = t // GRID_W
    return depthwise_conv(x.reshape(b * rows, GRID_W, c), w).reshape(b, t, c)

def conv_cols(x, w, layout):
    if layout == 'context':
        return depthwise_conv(x, w)
    b, t, c = x.shape
    rows = t // GRID_W
    xc = x.reshape(b, rows, GRID_W, c).transpose(0, 2, 1, 3).reshape(b * GRID_W, rows, c)
    y = depthwise_conv(xc, w)
    return y.reshape(b, GRID_W, rows, c).transpose(0, 2, 1, 3).reshape(b, t, c)

def gla_chunk_scan(q, k, v, log_f, s0):
    b, t, h, _ = q.shape
    dv = v.shape[-1]
    n = t // CHUNK

    def blocks(a):
        return a.reshape(b, n, CHUNK, h, a.shape[-1]).transpose(1, 0, 3, 2, 4)

    qc, kc, vc, gc = blocks(q), blocks(k), blocks(v), blocks(log_f)
    cum = jnp.cumsum(gc, axis=3)
    last = cum[:, :, :, -1:, :]
    causal = jnp.tril(jnp.ones((CHUNK, CHUNK), dtype=bool))[:, :, None]
    diff = cum[:, :, :, :, None, :] - cum[:, :, :, None, :, :]
    decay = jnp.where(causal, jnp.exp(jnp.where(causal, diff, 0.0)), 0.0)
    scores = jnp.einsum('nbhtk,nbhsk,nbhtsk->nbhts', qc, kc, decay)
    o_intra = jnp.einsum('nbhts,nbhsv->nbhtv', scores, vc)
    q_dec = qc * jnp.exp(cum)
    k_dec = kc * jnp.exp(last - cum)
    kv = jnp.einsum('nbhsk,nbhsv->nbhkv', k_dec, vc)
    chunk_decay = jnp.exp(last[:, :, :, 0, :])

    def step(s, inp):
        dec, kv_c = inp
        return dec[..., None] * s + kv_c, s

    s_final, s_before = lax.scan(step, s0.astype(jnp.float32), (chunk_decay, kv))
    o = o_intra + jnp.einsum('nbhtk,nbhkv->nbhtv', q_dec, s_before)
    return o.transpose(1, 0, 3, 2, 4).reshape(b, t, h, dv), s_final

def hgrn2_mixer(q_pre, i_pre, ff_pre, fb_pre, g_pre, lb_fwd, lb_bwd, gn_g, s0):
    b, t, _ = q_pre.shape

    def heads(a):
        return a.astype(jnp.float32).reshape(b, t, N_HEADS_C, -1)

    q = jax.nn.silu(heads(q_pre)) * (HEAD_K ** -0.5)
    v = heads(i_pre)

    def gates(f_pre, lb):
        x = heads(f_pre)
        lbh = lb.astype(jnp.float32).reshape(N_HEADS_C, HEAD_K)
        f = lbh + (1.0 - lbh) * jax.nn.sigmoid(x)
        return (1.0 - lbh) * jax.nn.sigmoid(-x), jnp.log(f)

    k_f, lf_f = gates(ff_pre, lb_fwd)
    k_b, lf_b = gates(fb_pre, lb_bwd)
    o_f, s_f = gla_chunk_scan(q, k_f, v, lf_f, s0[:, 0])
    flip = lambda a: jnp.flip(a, axis=1)
    o_b, s_b = gla_chunk_scan(flip(q), flip(k_b), flip(v), flip(lf_b), s0[:, 1])
    o = o_f + flip(o_b)
    o = o * lax.rsqrt(jnp.mean(o * o, axis=-1, keepdims=True) + EPS)
    o = o * gn_g.astype(jnp.float32).reshape(N_HEADS_C, HEAD_V)
    o = o.reshape(b, t, D_C) * jax.nn.silu(g_pre.astype(jnp.float32))
    return o.astype(q_pre.dtype), jnp.stack([s_f, s_b], axis=1)

def token_mix(h, w_in, w_out, conv_a_w, conv_b_w, conv_b_b, ln_g, ln_b, lb_fwd, lb_bwd, gn_g, s0, layout):
    proj = h @ w_in
    splits = [int(s) for s in np.cumsum(IN_WIDTHS)[:-1]]
    a_b, a_c, a_x, b_a, b_g, c_q, c_i, c_ff, c_fb, c_g = jnp.split(proj, splits, axis=-1)
    y_a = a_b * conv_rows(a_c * a_x, conv_a_w, layout)
    u = conv_cols(b_a * jax.nn.sigmoid(b_g), conv_b_w, layout) + conv_b_b
    y_b = jax.nn.silu(layer_norm(u, ln_g, ln_b))
    y_c, s_new = hgrn2_mixer(c_q, c_i, c_ff, c_fb, c_g, lb_fwd, lb_bwd, gn_g, s0)
    y = jnp.concatenate([y_a, y_b, y_c], axis=-1) @ w_out
    return y, s_new

def routed_moe(h, w_router, b_router, w_gate, w_up, w_down):
    b, t, d = h.shape
    hf = h.reshape(b * t, d)
    scores = jax.nn.softmax((hf @ w_router).astype(jnp.float32), axis=-1)
    biased = scores + b_router.astype(jnp.float32)
    group_score = lax.top_k(biased.reshape(-1, N_GROUPS, EXPERTS_PER_GROUP), GROUP_SCORE_K)[0].sum(-1)
    best = jnp.argmax(group_score, axis=-1)
    in_group = (jnp.arange(N_EXPERTS) // EXPERTS_PER_GROUP)[None, :] == best[:, None]
    _, idx = lax.top_k(jnp.where(in_group, biased, MASK_VALUE), TOP_K)
    w_sel = jnp.take_along_axis(scores, idx, axis=-1)
    w_sel = w_sel / jnp.sum(w_sel, axis=-1, keepdims=True)
    gates = jnp.einsum('nk,nke->ne', w_sel, jax.nn.one_hot(idx, N_EXPERTS, dtype=jnp.float32))
    hg = jnp.einsum('nd,edf->nef', hf, w_gate)
    hu = jnp.einsum('nd,edf->nef', hf, w_up)
    act = jax.nn.silu(hg) * hu * gates[:, :, None].astype(h.dtype)
    return jnp.einsum('nef,efd->nd', act, w_down).reshape(b, t, d)

def run_stream(x, cond, s_init, layout, lower_bound, norm_mix_g, norm_ffn_g, final_norm_g, w_ada, b_ada,
               w_in, w_out, conv_a_w, conv_b_w, conv_b_b, ln_b_g, ln_b_b, gnorm_c_g, w_router, b_router,
               w_gate, w_up, w_down):
    cond_act = jax.nn.silu(cond)
    states = []
    for l in range(DEPTH):
        mod = (cond_act @ w_ada[l] + b_ada[l])[:, None, :]
        sh1, sc1, g1, sh2, sc2, g2 = jnp.split(mod, N_MOD, axis=-1)
        h = rms_norm(x, norm_mix_g[l]) * (1 + sc1) + sh1
        y, s_new = token_mix(h, w_in[l], w_out[l], conv_a_w[l], conv_b_w[l], conv_b_b[l], ln_b_g[l], ln_b_b[l],
                             lower_bound[0, l], lower_bound[1, l], gnorm_c_g[l], s_init[:, l], layout)
        x = x + g1 * y
        if layout == 'context':
            states.append(s_new)
        h = rms_norm(x, norm_ffn_g[l]) * (1 + sc2) + sh2
        x = x + g2 * routed_moe(h, w_router, b_router, w_gate[l], w_up[l], w_down[l])
    y = rms_norm(x, final_norm_g)
    return y, (jnp.stack(states, axis=1) if states else None)

def setup_inputs(seed: int = 0) -> dict:
    key = jax.random.key(seed)
    ks = jax.random.split(key, 26)
    nrm = lambda k, shape, s: jax.random.normal(k, shape, jnp.float32) * s
    return {
        'x_prompt': nrm(ks[0], (BATCH, SEQ, D_MODEL), 1.0),
        'x_sample': nrm(ks[1], (DEC_BATCH, DEC_SEQ, D_MODEL), 1.0),
        'state_hgrn': nrm(ks[2], (DEC_BATCH, DEPTH, 2, N_HEADS_C, HEAD_K, HEAD_V), 0.5),
        'c': nrm(ks[3], (DEC_BATCH, D_MODEL), 1.0),
        'c_ctx': nrm(ks[4], (D_MODEL,), 1.0),
        'norm_mix_g': 1.0 + nrm(ks[5], (DEPTH, D_MODEL), 0.02),
        'norm_ffn_g': 1.0 + nrm(ks[6], (DEPTH, D_MODEL), 0.02),
        'final_norm_g': 1.0 + nrm(ks[7], (D_MODEL,), 0.02),
        'w_ada': nrm(ks[8], (DEPTH, D_MODEL, N_MOD * D_MODEL), 0.5 * D_MODEL ** -0.5),
        'b_ada': nrm(ks[9], (DEPTH, N_MOD * D_MODEL), 0.02),
        'w_in': nrm(ks[10], (DEPTH, D_MODEL, D_IN), D_MODEL ** -0.5),
        'w_out': nrm(ks[11], (DEPTH, D_MIX, D_MODEL), D_MIX ** -0.5),
        'conv_a_w': nrm(ks[12], (DEPTH, CONV_A, D_A), CONV_A ** -0.5),
        'conv_b_w': nrm(ks[13], (DEPTH, CONV_B, D_B), CONV_B ** -0.5),
        'conv_b_b': nrm(ks[14], (DEPTH, D_B), 0.02),
        'ln_b_g': 1.0 + nrm(ks[15], (DEPTH, D_B), 0.02),
        'ln_b_b': nrm(ks[16], (DEPTH, D_B), 0.02),
        'lb_logits': nrm(ks[17], (2, DEPTH, D_C), 0.5),
        'gnorm_c_g': 1.0 + nrm(ks[18], (DEPTH, D_C), 0.02),
        'w_router': nrm(ks[19], (D_MODEL, N_EXPERTS), D_MODEL ** -0.5),
        'b_router': nrm(ks[20], (N_EXPERTS,), 0.01),
        'w_gate': nrm(ks[21], (DEPTH, N_EXPERTS, D_MODEL, D_EXPERT), D_MODEL ** -0.5),
        'w_up': nrm(ks[22], (DEPTH, N_EXPERTS, D_MODEL, D_EXPERT), D_MODEL ** -0.5),
        'w_down': nrm(ks[23], (DEPTH, N_EXPERTS, D_EXPERT, D_MODEL), D_EXPERT ** -0.5),
    }

def reference(x_prompt, x_sample, state_hgrn, c, c_ctx, norm_mix_g, norm_ffn_g, final_norm_g, w_ada, b_ada,
              w_in, w_out, conv_a_w, conv_b_w, conv_b_b, ln_b_g, ln_b_b, lb_logits, gnorm_c_g, w_router,
              b_router, w_gate, w_up, w_down):
    p = jax.nn.softmax(lb_logits.astype(jnp.float32), axis=1)
    lower_bound = jnp.cumsum(p, axis=1) - p[:, :1]
    s_zero = jnp.zeros((x_prompt.shape[0], DEPTH, 2, N_HEADS_C, HEAD_K, HEAD_V), jnp.float32)
    y_prompt, new_state_hgrn = run_stream(
        x_prompt, c_ctx[None, :], s_zero, 'context', lower_bound, norm_mix_g, norm_ffn_g, final_norm_g,
        w_ada, b_ada, w_in, w_out, conv_a_w, conv_b_w, conv_b_b, ln_b_g, ln_b_b, gnorm_c_g, w_router,
        b_router, w_gate, w_up, w_down)
    y_sample, _ = run_stream(
        x_sample, c, state_hgrn, 'latent', lower_bound, norm_mix_g, norm_ffn_g, final_norm_g,
        w_ada, b_ada, w_in, w_out, conv_a_w, conv_b_w, conv_b_b, ln_b_g, ln_b_b, gnorm_c_g, w_router,
        b_router, w_gate, w_up, w_down)
    return (y_prompt, y_sample, new_state_hgrn)


_drawn_inputs = setup_inputs


def setup_inputs(seed=0):
    import zlib

    import numpy as np

    out = dict(_drawn_inputs(seed))
    spreads = {}
    factors = {'state_hgrn': 36.969,
     'norm_mix_g': 2.692,
     'norm_ffn_g': 3.11,
     'final_norm_g': 8.132,
     'conv_b_b': 3.428,
     'ln_b_g': 8.0,
     'ln_b_b': 5.768,
     'gnorm_c_g': 5.876}
    for name, (base, spread) in spreads.items():
        noise = np.random.default_rng([zlib.crc32(name.encode()), seed]).standard_normal(out[name].shape)
        drawn = base * np.exp(spread * noise) if base else spread * noise
        out[name] = __import__('jax').numpy.asarray(drawn.astype(out[name].dtype))
    for name, factor in factors.items():
        out[name] = (out[name] * factor).astype(out[name].dtype)
    return out
```

```python
from contextlib import ExitStack

import concourse.bass as bass
from concourse import mybir

F32 = mybir.dt.float32
F32R = mybir.dt.float32r
I32 = mybir.dt.int32
U8 = mybir.dt.uint8
ALU = mybir.AluOpType
ACT = mybir.ActivationFunctionType
AX = mybir.AxisListType.X

P = 128
D = 1024
J = D // P
CTX, LAT, GRID_W = 128, 256, 64
TOK = CTX + LAT
NT = TOK // P
COND = [0, 1, 1]
HEADS = 4
HW = HEADS * TOK
CONV_A, CONV_B = 3, 31
NROW = CONV_A + CONV_B + 3
LEVELS = 7
EXPERTS, GROUPS, PER_GROUP = 16, 4, 4
FE = 512
EPS = 1e-6
TAPS_B = [("middle", 0)] + [("time", d) for d in range(-15, 16) if d] + [("column", r) for r in range(-3, 4) if r]
NTAPB = len(TAPS_B)
NCHAIN = 19
CHUNK = 1024

NRAW = 8
NSPLIT = 4

COL = dict(ab=0, ac=256, ax=512, ba=768, bg=1024, q=1280, i=1792, ff=2304, fb=2816, g=3328)
WIN = ([("ff", h) for h in range(4)] + [("fb", h) for h in range(4)] + [("q", h) for h in range(4)]
       + [("i", h) for h in range(4)] + [("bg", 0), ("bg", 1), ("ba", 0), ("ba", 1)]
       + [("g", h) for h in range(4)] + [("ac", 0), ("ac", 1), ("ax", 0), ("ax", 1), ("ab", 0), ("ab", 1)])
NWIN = len(WIN)
WOUT = [0, 1, 4, 5, 6, 7, 2, 3]
SC1, SH1, G1, SH2, SC2, G2 = range(6)
ADA = [(1, 0), (0, 1), (2, 2), (3, 3), (4, 0), (5, 1)]


def front_chunks():
    ada = [("ada", a, half, i) for a in range(6) for half in range(2) for i in range(4)]
    out, ada = ada[:16], ada[16:]
    for n in range(NWIN):
        out.append(("win", n))
        take = 2 if n < 6 else 1 if n < 26 else 0
        out, ada = out + ada[:take], ada[take:]
    assert not ada
    return out + [("wout", k) for k in range(8)]


FRONT = front_chunks()
SPLIT_OF = {c: n for n, c in enumerate(x for x in FRONT if x[0] != "ada")}
NFRONT, NFS = len(FRONT), len(SPLIT_OF)
STAGES = [("G", 0), ("U", 0), ("G", 1), ("U", 1), ("D", 0), ("G", 2), ("U", 2), ("D", 1), ("G", 3), ("U", 3),
          ("D", 2), ("D", 3)]
NG = 4 * len(STAGES)
AHEAD = NSPLIT - 1

COMBINE_AFTER = [3, 5, 7]
TURN_AFTER = 9
GATHER_AFTER = [21, 23]
SPREAD_AFTER = [42, 44]
SLOT_GATE_AFTER = 45


def stage_end(what, e):
    return 4 * STAGES.index((what, e)) + 4


AT_AFTER = [4 * STAGES.index(("D", e)) - 3 for e in range(PER_GROUP)]
assert NG % NRAW == 0 and NG % NSPLIT == 0
assert all(x[0] != "ada" for x in FRONT[-NRAW:])


def act_ops(kind):
    return {"ff": (2, 0), "fb": (2, 0), "q": (1, 1), "bg": (1, 0), "ba": (0, 1), "g": (1, 1),
            "ac": (1, 0), "ax": (0, 1), "ab": (1, 0)}[kind]


def evac_counts():
    a = d = 0
    out = []
    for kind, h in WIN:
        if kind == "i":
            a += 3 if h == 3 else 0
        else:
            x, y = act_ops(kind)
            a, d = a + x, d + y
        out.append((a, d))
    return out


EVAC = evac_counts()


def build(nc, x_prompt, x_sample, state_hgrn, c, c_ctx, norm_mix_g, norm_ffn_g, final_norm_g, w_ada, b_ada,
          w_in, w_out, conv_a_w, conv_b_w, conv_b_b, ln_b_g, ln_b_b, lb_logits, gnorm_c_g, w_router,
          b_router, w_gate, w_up, w_down, y_prompt, y_sample, new_state):
    ctx = ExitStack()
    with ctx:
        def sb(name, shape, dt=F32):
            return ctx.enter_context(nc.sbuf_tensor(name, shape, dt))

        def sem(name):
            return ctx.enter_context(nc.semaphore(name))

        raw = sb("raw", [P, NRAW, CHUNK])
        whi = sb("whi", [P, NSPLIT, CHUNK], F32R)
        wlo = sb("wlo", [P, NSPLIT, CHUNK], F32R)
        lhs_hi = sb("lhs_hi", [P, 8 * TOK], F32R)
        lhs_lo = sb("lhs_lo", [P, 8 * TOK], F32R)
        xres = sb("xres", [P, NT, D])
        part = sb("part", [P, 4, D])
        ident = sb("ident", [P, P])
        ones = sb("ones", [P, P])
        sel_t = sb("sel_t", [P, 2])
        sel_b = sb("sel_b", [P, 2, P])
        upper = sb("upper", [P, P])
        iota_row = sb("iota_row", [P, P])
        masks = sb("masks", [P, LEVELS, P], U8)
        csel = sb("csel", [P, J, 32])
        craw = sb("craw", [P, 2, J])
        csig = sb("csig", [P, 2, J])
        gmix = sb("gmix", [P, J])
        bada = sb("bada", [P, 2, J])
        scl = sb("scl", [P, J, 2])
        shf = sb("shf", [P, J, 2])
        ct = sb("ct", [P, 2, NROW])
        gt = sb("gt", [P, 12])
        lbt = sb("lbt", [P, 4, 8])
        eps = sb("eps", [P, 1])
        ssq = sb("ssq", [P, 3, NT])
        std = sb("std", [P, 3, NT])
        rstd = sb("rstd", [P, 3, NT])
        wr = sb("wr", [P, J, EXPERTS])
        brt = sb("brt", [P, EXPERTS])
        gidx = sb("gidx", [P, GROUPS])
        eidx = sb("eidx", [P, EXPERTS])
        goff = sb("goff", [P, GROUPS])
        base_it = sb("base_it", [P, 4 * GROUPS])
        flag = sb("flag", [P, 1], I32)
        flagf = sb("flagf", [P, 1])

        FIRST, SECOND = 36 * 256, 45 * 256
        with ExitStack() as front:
            area1 = front.enter_context(nc.sbuf_tensor("front1", [P, FIRST], F32))
            area2 = front.enter_context(nc.sbuf_tensor("front2", [P, SECOND], F32))
        with ExitStack() as chain:
            rows = chain.enter_context(nc.sbuf_tensor("rows", [P, 6 * D], F32))
        ys_h = sb("ys_h", [P, D], F32R)
        ys_l = sb("ys_l", [P, D], F32R)
        at_hi = sb("at_hi", [P, 2, 4, P], F32R)
        at_lo = sb("at_lo", [P, 2, 4, P], F32R)
        hgf = sb("hgf", [P, D])
        area3 = sb("back1", [P, FIRST - 5 * D])
        hg_hi = sb("hg_hi", [P, J, P], F32R)
        hg_lo = sb("hg_lo", [P, J, P], F32R)
        place = sb("place", [P, NT, P], F32R)
        place_t = sb("place_t", [P, NT, P], F32R)
        area4 = sb("back2", [P, SECOND - (2 * J + 6) * P])

        def cut(area, at, *shape):
            n = 1
            for s in shape:
                n *= s
            v = area[:, at:at + n]
            if len(shape) == 2:
                return v.rearrange("p (a b) -> p a b", b=shape[1])
            if len(shape) == 3:
                return v.rearrange("p (a b c) -> p a b c", b=shape[1], c=shape[2])
            return v

        aq = cut(area1, 0, 2, HEADS, TOK)
        v_tok = cut(area1, 2 * HW, NT, HEADS * P)
        smat = cut(area1, 2 * HW + NT * 512, NT, HEADS, P)
        tot_f = cut(area1, 2 * HW + NT * 1024, HEADS, TOK)
        tot_b = cut(area1, 3 * HW + NT * 1024, HEADS, TOK)
        ak = cut(area2, 0, 2, HEADS, TOK)
        ff = cut(area2, 2 * HW, HEADS, TOK)
        fb = cut(area2, 3 * HW, HEADS, TOK)
        qh = cut(area2, 4 * HW, HEADS, TOK)
        ksum = cut(area2, 5 * HW, HEADS, TOK)
        ya = cut(area2, 5 * HW, 2, TOK)
        yb = cut(area2, 5 * HW + 2 * TOK, 2, TOK)
        ua = cut(area2, 6 * HW, 2, TOK)
        ab = cut(area2, 6 * HW + 2 * TOK, 2, TOK)
        ub = cut(area2, 6 * HW + 4 * TOK, 2, TOK)
        assert 6 * HW + 6 * TOK <= SECOND
        kt = cut(area2, 0, 4, HEADS, P)
        hn = cut(area2, 4 * 512, 2, TOK)
        s0 = cut(area2, 3 * HW, 2, HEADS * P)
        st_out_f = area2[:, 3 * HW + 1024:3 * HW + 1536]
        sf2 = cut(area2, 2 * HW, HEADS, P)
        sb1 = cut(area2, 2 * HW + 512, HEADS, P)
        st_out_b = area2[:, 2 * HW + 1024:2 * HW + 1536]
        xnt = cut(area2, 0, J, TOK)
        xn = cut(area1, 0, NT, D)
        junk = area1[:, NT * D:NT * D + D]
        int_a = area1[:, 5 * D:5 * D + P].bitcast(I32)
        int_b = area1[:, 5 * D + P:5 * D + 2 * P].bitcast(I32)
        int_c = area1[:, 5 * D + 2 * P:5 * D + 3 * P].bitcast(I32)
        cw = area1[:, 6 * D:6 * D + 256]
        gw = area1[:, 6 * D + 256:6 * D + 384]

        row_g1 = cut(rows, 0, 2, D)
        row_sh2 = cut(rows, 2 * D, 2, D)
        row_sc2 = cut(rows, 4 * D, 2, D)
        row_g2 = cut(area3, D, 2, D)
        row_g = area3[:, 3 * D:4 * D]
        h2 = cut(area4, 0, NT, D)
        h2t = cut(area4, NT * D, J, TOK)
        acc = cut(area4, NT * D, NT, D)
        sgate = area4[:, 0:FE]
        eact = area4[:, FE:2 * FE]
        y3 = cut(area4, 0, NT, D)
        rt = sb("rt", [P, 15, NT, EXPERTS])
        rpair = sb("rpair", [P, NT * GROUPS, 6])
        code = sb("code", [P, NT])
        codem = sb("codem", [P, NT, 4 * GROUPS])
        gates = sb("gates", [P, NT, EXPERTS + PER_GROUP])
        gsel4 = sb("gsel4", [P, NT, PER_GROUP])
        gate4 = sb("gate4", [P, PER_GROUP])

        bank = [ctx.enter_context(nc.psum_tensor(f"bank{i}", [P, 512], F32)) for i in range(8)]

        x_landed = [sem(f"x_landed{t}") for t in range(NT)]
        cond_landed, small_landed, rows_landed = sem("cond_landed"), sem("small_landed"), sem("rows_landed")
        w_landed = [sem(f"w_landed{i}") for i in range(NRAW)]
        state_landed, ffn_g_landed, final_g_landed = sem("state_landed"), sem("ffn_g_landed"), sem("final_g_landed")
        bias_landed = [sem(f"bias_landed{i}") for i in range(4)]
        state_stored, y_stored = sem("state_stored"), sem("y_stored")
        consts, const_step, masks_ready = sem("consts"), sem("const_step"), sem("masks_ready")
        act_step, vec_step, pool_step = sem("act_step"), sem("vec_step"), sem("pool_step")
        hi_ready, lo_ready, w_used = sem("hi_ready"), sem("lo_ready"), sem("w_used")
        ada_used, ada_evac, mod_ready, mod_done = sem("ada_used"), sem("ada_evac"), sem("mod_ready"), sem("mod_done")
        csig_ready, csel_ready = sem("csig_ready"), sem("csel_ready")
        std_ready, rstd_ready, xn_ready = sem("std_ready"), sem("rstd_ready"), sem("xn_ready")
        ssq_ready = sem("ssq_ready")
        par_ready, par_evac, lb_ready = sem("par_ready"), sem("par_evac"), sem("lb_ready")
        xt_ready, xt_evac = sem("xt_ready"), sem("xt_evac")
        h_ready, h_hi, h_lo = sem("h_ready"), sem("h_hi"), sem("h_lo")
        proj_act, proj_dve = sem("proj_act"), sem("proj_dve")
        gates_ready, tots_ready, prep_ready = sem("gates_ready"), sem("tots_ready"), sem("prep_ready")
        kc_ready, score_ready, s_merged = sem("kc_ready"), sem("score_ready"), sem("s_merged")
        q_step, k_step = sem("q_step"), sem("k_step")
        kt_ready, kt_evac, kv_ready, kv_out, state_ready = (sem("kt_ready"), sem("kt_evac"), sem("kv_ready"),
                                                            sem("kv_out"), sem("state_ready"))
        convb_step, conva_step = sem("convb_step"), sem("conva_step")
        ln_mean, ln_centred, ln_sq, ln_var, ln_std, ln_norm, ln_sig = (
            sem("ln_mean"), sem("ln_centred"), sem("ln_sq"), sem("ln_var"), sem("ln_std"), sem("ln_norm"),
            sem("ln_sig"))
        o_ready, o_sq, o_sum, o_std, o_norm = sem("o_ready"), sem("o_sq"), sem("o_sum"), sem("o_std"), sem("o_norm")
        y_hi, y_lo = sem("y_hi"), sem("y_lo")
        row_ready, row_act, row_dve = sem("row_ready"), sem("row_act"), sem("row_dve")
        x2_ready, h2_ready, h2t_ready, h2t_evac = sem("x2_ready"), sem("h2_ready"), sem("h2t_ready"), sem("h2t_evac")
        h2_hi, h2_lo = sem("h2_hi"), sem("h2_lo")
        logits_ready, shifted, exp_ready = sem("logits_ready"), sem("shifted"), sem("exp_ready")
        group_ready, rank_ready, flag_ready = sem("group_ready"), sem("rank_ready"), sem("flag_ready")
        place_ready, gather_ready, gather_evac = sem("place_ready"), sem("gather_ready"), sem("gather_evac")
        spread_ready, hg_hi_ready, hg_lo_ready = sem("spread_ready"), sem("hg_hi_ready"), sem("hg_lo_ready")
        slot_gate, slot_gate_evac, turn_ready, turn_evac = (sem("slot_gate"), sem("slot_gate_evac"),
                                                            sem("turn_ready"), sem("turn_evac"))
        silu_ready, eact_ready, at_ready, at_hi_ready, at_lo_ready = (
            sem("silu_ready"), sem("eact_ready"), sem("at_ready"), sem("at_hi_ready"), sem("at_lo_ready"))
        ys_hi, ys_lo, comb_ready, comb_added = sem("ys_hi"), sem("ys_lo"), sem("comb_ready"), sem("comb_added")
        acc_zero, place_t_zero, x3_ready, y_ready = sem("acc_zero"), sem("place_t_zero"), sem("x3_ready"), sem("y_ready")

        ada_v = w_ada[0].rearrange("(p j) n -> p j n", j=J)
        win_v = w_in[0].rearrange("(p j) n -> p j n", j=J)
        x_tiles = [x_prompt[0], x_sample[0, 0:P, :], x_sample[0, P:2 * P, :]]
        y_tiles = [y_prompt[0], y_sample[0, 0:P, :], y_sample[0, P:2 * P, :]]

        def spread(vec, n):
            return bass.AP(vec.tensor, vec.offset, [[0, P], [1, n]])

        def front_source(x):
            if x[0] == "ada":
                _, a, half, i = x
                n0 = ADA[a][0] * D + half * 512
                return ada_v[:, 2 * i:2 * i + 2, n0:n0 + 512], 512
            if x[0] == "win":
                kind, h = WIN[x[1]]
                if kind == "i":
                    return win_v[:, 2 * h:2 * h + 2, COL["i"]:COL["i"] + 512], 512
                n0 = COL[kind] + h * P
                return win_v[:, :, n0:n0 + P], P
            m = WOUT[x[1]]
            return w_out[0, m * P:(m + 1) * P, :].rearrange("p (a n) -> p a n", a=1), CHUNK

        def raw_as(slot, inner):
            return raw[:, slot, :].rearrange("p (a n) -> p a n", n=inner)

        def raw_slot(local):
            return (NFRONT + local) % NRAW

        def split_slot(local):
            return (NFS + local) % NSPLIT

        def load_front(sp):
            for n, x in enumerate(FRONT):
                if n >= NRAW:
                    old = FRONT[n - NRAW]
                    if old[0] == "ada":
                        sp.wait_ge(ada_used, sum(y[0] == "ada" for y in FRONT[:n - NRAW + 1]))
                    else:
                        sp.wait_ge(lo_ready, SPLIT_OF[old] + 1)
                src, inner = front_source(x)
                sp.dma_start(raw_as(n % NRAW, inner), src).then_inc(w_landed[n % NRAW], 16)

        def load_group(sp, it, g):
            for k, (what, e) in enumerate(STAGES):
                for i in range(4):
                    n = 4 * k + i
                    sp.wait_ge(lo_ready, it * NG + (NFS + n - NRAW + 1))
                    src = {"G": w_gate, "U": w_up, "D": w_down}[what][0, bass.ds(g * PER_GROUP + e, 1)]
                    if what == "D":
                        src = src.rearrange("o (p j) d -> (o p) j d", j=4)[:, i:i + 1, :]
                        dst = raw_as(raw_slot(n), CHUNK)
                    else:
                        src = src.rearrange("o (p j) f -> (o p) j f", j=J)[:, 2 * i:2 * i + 2, :]
                        dst = raw_as(raw_slot(n), FE)
                    sp.dma_start(dst, src).then_inc(w_landed[raw_slot(n)], 16)

        def overflow(eng):
            eng.wait_ge(flag_ready, 1)
            return eng.value_load(flag[0:1, 0:1], min_val=0, max_val=1) > 0

        def experts(eng, one_group):
            with eng.Fori(0, GROUPS) as g:
                one_group(eng, g, g)
            with eng.If(overflow(eng)):
                with eng.Fori(1, 3) as turn:
                    with eng.Fori(0, GROUPS) as g:
                        one_group(eng, turn * GROUPS + g, g)

        def passes(eng):
            return eng.value_load(flag[0:1, 0:1], min_val=0, max_val=1) * (2 * GROUPS) + GROUPS

        def totals(tot, lev):
            n = TOK >> lev
            return tot[:, :, TOK - 2 * n:TOK - n]

        def halves(a, lev):
            return a.rearrange("p h (n two w) -> p h n two w", two=2, w=1 << lev)

        def block_total(one, tot, lev, half):
            src = one if lev == 0 else totals(tot, lev)
            v = src.rearrange("p h (n two) -> p h n two", two=2)[:, :, :, half]
            n = TOK >> (lev + 1)
            return v.rearrange("p h (n o) -> p h n o", o=1).broadcast_to([P, HEADS, n, 1 << lev])

        def three(pe, out, a_hi, a_lo, b_hi, b_lo, first, last):
            pe.matmul(out, a_hi, b_hi, start=first, stop=False)
            pe.matmul(out, a_hi, b_lo, start=False, stop=False)
            return pe.matmul(out, a_lo, b_hi, start=False, stop=last)

        def vec_place(dve, it, g):
            for t in range(NT):
                dve.tensor_scalar(place[:, t, :], iota_row[:], codem[:, t, bass.ds(it, 1)], None, ALU.is_equal)\
                    .then_inc(place_ready, 1)
            dve.tensor_copy(gsel4[:], gates[:, :, bass.ds(g * PER_GROUP, PER_GROUP)]).then_inc(place_ready, 1)

        def pe_gather(pe, it, half, first=False):
            if half == 0:
                pe.wait_ge(place_ready, it * 4 + 4)
                if not first:
                    pe.wait_ge(comb_added, it * 6)
            for t in range(NT):
                x = slice(t * D + half * 512, t * D + (half + 1) * 512)
                pe.matmul(bank[6 + half][:], place[:, t, :], lhs_hi[:, x], start=(t == 0), stop=False)
                last = pe.matmul(bank[6 + half][:], place[:, t, :], lhs_lo[:, x], start=False, stop=(t == NT - 1))
            last.then_inc(gather_ready, 1)

        def act_gather(act, it, half):
            act.wait_ge(gather_ready, it * 2 + (half + 1))
            act.activation(hgf[:, half * 512:(half + 1) * 512], bank[6 + half][:], ACT.Copy)\
                .then_inc(gather_evac, 1)

        def pe_spread(pe, it, half, first=False):
            pe.wait_ge(gather_evac, it * 2 + (half + 1))
            if not first:
                pe.wait_ge(silu_ready, it * PER_GROUP)
            for jj in range(4):
                j = 4 * half + jj
                last = pe.transpose(bank[half][:, jj * P:(jj + 1) * P], hgf[:, j * P:(j + 1) * P], ident[:])
            last.then_inc(spread_ready, 1)

        def act_spread(act, it, half):
            act.wait_ge(spread_ready, it * 2 + (half + 1))
            act.activation(hg_hi[:, 4 * half:4 * half + 4, :], bank[half][:].rearrange("p (j t) -> p j t", j=4),
                           ACT.Copy).then_inc(hg_hi_ready, 1)

        def vec_spread(dve, it, half):
            dve.wait_ge(hg_hi_ready, it * 2 + (half + 1))
            dve.tensor_tensor(hg_lo[:, 4 * half:4 * half + 4, :], bank[half][:].rearrange("p (j t) -> p j t", j=4),
                              hg_hi[:, 4 * half:4 * half + 4, :].bitcast(F32), ALU.subtract)\
                .then_inc(hg_lo_ready, 1)

        def pe_slot_gate(pe, it, first=False):
            if not first:
                pe.wait_ge(at_lo_ready, it * PER_GROUP)
            for t in range(NT):
                last = pe.matmul(bank[3][:, 0:PER_GROUP], place[:, t, :].bitcast(F32), gsel4[:, t, :],
                                 start=(t == 0), stop=(t == NT - 1))
            last.then_inc(slot_gate, 1)

        def vec_slot_gate(dve, it):
            dve.wait_ge(slot_gate, it + 1)
            dve.tensor_copy(gate4[:], bank[3][:, 0:PER_GROUP]).then_inc(slot_gate_evac, 1)

        def act_output(act, it):
            act.wait_ge(w_used, it * NG + NFS)
            for half in range(2):
                act.activation(ys_h[:, half * 512:(half + 1) * 512], bank[4 + half][:], ACT.Copy).then_inc(ys_hi, 1)

        def vec_output(dve, it):
            for half in range(2):
                cols = slice(half * 512, (half + 1) * 512)
                dve.wait_ge(ys_hi, it * 2 + (half + 1))
                dve.tensor_tensor(ys_l[:, cols], bank[4 + half][:], ys_h[:, cols].bitcast(F32), ALU.subtract)\
                    .then_inc(ys_lo, 1)

        def pe_combine(pe, it, t):
            if t == 0:
                pe.wait_ge(ys_lo, it * 2 + 2)
            for half in range(2):
                if t:
                    pe.wait_ge(comb_added, it * 6 + (2 * t + half - 1))
                cols = slice(half * 512, (half + 1) * 512)
                pe.matmul(bank[6 + half][:], place_t[:, t, :], ys_h[:, cols], start=True, stop=False)
                pe.matmul(bank[6 + half][:], place_t[:, t, :], ys_l[:, cols], start=False, stop=True)\
                    .then_inc(comb_ready, 1)

        def vec_combine(dve, it, t):
            for half in range(2):
                cols = slice(half * 512, (half + 1) * 512)
                dve.wait_ge(comb_ready, it * 6 + (2 * t + half + 1))
                dve.tensor_tensor(acc[:, t, cols], acc[:, t, cols], bank[6 + half][:], ALU.add)\
                    .then_inc(comb_added, 1)

        def act_group(act, it, g):
            def high(n):
                if n < NG:
                    act.wait_ge(w_landed[raw_slot(n)], it * (16 * NG // NRAW) + 16 * ((NFRONT + n) // NRAW + 1))
                    act.wait_ge(w_used, it * NG + (NFS + n - NSPLIT + 1))
                    act.activation(whi[:, split_slot(n), :], raw[:, raw_slot(n), :], ACT.Copy).then_inc(hi_ready, 1)

            for n in range(AHEAD):
                high(n)
            act_output(act, it)
            for n in range(NG):
                high(n + AHEAD)
                for e in range(PER_GROUP):
                    if n == stage_end("G", e):
                        act.wait_ge(w_used, it * NG + (NFS + n))
                        if e:
                            act.wait_ge(eact_ready, it * PER_GROUP + e)
                        act.activation(sgate, bank[e % 2][:], ACT.Silu).then_inc(silu_ready, 1)
                    if n == AT_AFTER[e] + 1:
                        act.wait_ge(at_ready, it * PER_GROUP + (e + 1))
                        act.activation(at_hi[:, e % 2], bank[3][:].rearrange("p (j s) -> p j s", j=4), ACT.Copy)\
                            .then_inc(at_hi_ready, 1)
                if n == TURN_AFTER + 1:
                    act.wait_ge(turn_ready, it + 1)
                    act.activation(place_t[:], bank[3][:, 0:TOK].rearrange("p (t s) -> p t s", t=NT), ACT.Copy)\
                        .then_inc(turn_evac, 1)
                for half in range(2):
                    if n == GATHER_AFTER[half] + 1:
                        act_gather(act, it + 1, half)
                    if n == SPREAD_AFTER[half] + 1:
                        act_spread(act, it + 1, half)

        def pe_group(pe, it, g):
            for n in range(NG):
                k, i = divmod(n, 4)
                what, e = STAGES[k]
                if what == "G" and e >= 2 and i == 0:
                    pe.wait_ge(silu_ready, it * PER_GROUP + (e - 1))
                if what == "U" and i == 0 and e:
                    pe.wait_ge(eact_ready, it * PER_GROUP + e)
                if what == "D" and i == 0:
                    pe.wait_ge(at_lo_ready, it * PER_GROUP + (e + 1))
                slot = split_slot(n)
                pe.wait_ge(lo_ready, it * NG + (NFS + n + 1))
                if what == "D":
                    for half in range(2):
                        w = slice(half * 512, (half + 1) * 512)
                        last = three(pe, bank[4 + half][:], at_hi[:, e % 2, i, :], at_lo[:, e % 2, i, :],
                                     whi[:, slot, w], wlo[:, slot, w], e == 0 and i == 0, e == 3 and i == 3)
                else:
                    if k == 0:
                        pe.wait_ge(hg_lo_ready, it * 2 + (i // 2 + 1))
                    out = bank[e % 2] if what == "G" else bank[2]
                    for jj in range(2):
                        j = 2 * i + jj
                        w = slice(jj * 512, (jj + 1) * 512)
                        last = three(pe, out[:], hg_hi[:, j, :], hg_lo[:, j, :], whi[:, slot, w],
                                     wlo[:, slot, w], j == 0, j == J - 1)
                last.then_inc(w_used, 1)
                for t in range(NT):
                    if n == COMBINE_AFTER[t]:
                        pe_combine(pe, it, t)
                if n == TURN_AFTER:
                    pe.wait_ge(slot_gate_evac, it + 1)
                    for t in range(NT):
                        last = pe.transpose(bank[3][:, t * P:(t + 1) * P], place[:, t, :].bitcast(F32), ident[:])
                    last.then_inc(turn_ready, 1)
                for half in range(2):
                    if n == GATHER_AFTER[half]:
                        pe_gather(pe, it + 1, half)
                for e in range(PER_GROUP):
                    if n == AT_AFTER[e]:
                        pe.wait_ge(eact_ready, it * PER_GROUP + (e + 1))
                        if e == 0:
                            pe.wait_ge(turn_evac, it + 1)
                        for j in range(4):
                            last = pe.transpose(bank[3][:, j * P:(j + 1) * P], eact[:, j::4], ident[:])
                        last.then_inc(at_ready, 1)
                for half in range(2):
                    if n == SPREAD_AFTER[half]:
                        pe_spread(pe, it + 1, half)
                if n == SLOT_GATE_AFTER:
                    pe_slot_gate(pe, it + 1)

        def vec_group(dve, it, g):
            def low(n):
                if n < NG:
                    dve.wait_ge(hi_ready, it * NG + (NFS + n + 1))
                    dve.tensor_tensor(wlo[:, split_slot(n), :], raw[:, raw_slot(n), :],
                                      whi[:, split_slot(n), :].bitcast(F32), ALU.subtract).then_inc(lo_ready, 1)

            for n in range(AHEAD):
                low(n)
            vec_output(dve, it)
            for n in range(NG):
                low(n + AHEAD)
                for t in range(NT):
                    if n == COMBINE_AFTER[t] + 1:
                        vec_combine(dve, it, t)
                if n == TURN_AFTER + 4:
                    dve.wait_ge(turn_ready, it + 1)
                    vec_place(dve, it + 1, g + 1)
                for e in range(PER_GROUP):
                    if n == stage_end("U", e):
                        dve.wait_ge(w_used, it * NG + (NFS + n))
                        dve.wait_ge(silu_ready, it * PER_GROUP + (e + 1))
                        if e:
                            dve.wait_ge(at_ready, it * PER_GROUP + e)
                        dve.scalar_tensor_tensor(out=eact, in0=bank[2][:], scalar=gate4[:, e:e + 1], in1=sgate,
                                                 op0=ALU.mult, op1=ALU.mult).then_inc(eact_ready, 1)
                    if n == AT_AFTER[e] + 1:
                        dve.wait_ge(at_hi_ready, it * PER_GROUP + (e + 1))
                        dve.tensor_tensor(at_lo[:, e % 2], bank[3][:].rearrange("p (j s) -> p j s", j=4),
                                          at_hi[:, e % 2].bitcast(F32), ALU.subtract).then_inc(at_lo_ready, 1)
                for half in range(2):
                    if n == SPREAD_AFTER[half] + 1:
                        vec_spread(dve, it + 1, half)
                if n == SLOT_GATE_AFTER + 1:
                    vec_slot_gate(dve, it + 1)
            dve.wait_ge(slot_gate_evac, it + 2)
            dve.wait_ge(comb_added, it * 6 + 6)

        block = ctx.enter_context(nc.Block())

        @block.sync
        def _(sp):
            load_front(sp)
            experts(sp, load_group)
            for t in range(NT):
                sp.wait_ge(y_ready, t + 1)
                sp.dma_start(y_tiles[t], y3[:, t, :]).then_inc(y_stored, 16)
            sp.wait_ge(y_stored, 16 * NT)
            sp.wait_ge(state_stored, 32)

        @block.gpsimd
        def _(pool):
            n = [0]

            def chain(ins):
                n[0] += 1
                ins.then_inc(const_step, 1)
                pool.wait_ge(const_step, n[0])

            chain(pool.memset(ident[:], 0.0))
            pool.affine_select(out=ident[:], in_=ident[:], compare_op=ALU.not_equal, fill=1.0, base=0,
                               pattern=[[-1, P]], channel_multiplier=1).then_inc(consts, 1)
            pool.memset(ones[:], 1.0).then_inc(consts, 1)
            pool.memset(eps[:], EPS).then_inc(consts, 1)
            chain(pool.memset(sel_t[:], 0.0))
            for q in range(4):
                chain(pool.affine_select(out=sel_t[:], in_=sel_t[:], compare_op=ALU.not_equal, fill=1.0,
                                         base=-32 * q, pattern=[[-1, 2]], channel_multiplier=1))
            chain(pool.memset(sel_b[:], 0.0))
            for cond in range(2):
                for row in [32 * q + cond for q in range(4)] + [2]:
                    chain(pool.affine_select(out=sel_b[:, cond, :], in_=sel_b[:, cond, :],
                                             compare_op=ALU.not_equal, fill=1.0, base=-row,
                                             pattern=[[0, P]], channel_multiplier=1))
            chain(pool.iota(int_a, [[1, P]], base=0, channel_multiplier=0))
            chain(pool.iota(int_b, [[0, P]], base=0, channel_multiplier=1))
            pool.memset(upper[:], 1.0).then_inc(consts, 1)
            pool.wait_ge(consts, 4)
            pool.affine_select(out=upper[:], in_=upper[:], compare_op=ALU.is_ge, fill=0.0, base=-1,
                               pattern=[[1, P]], channel_multiplier=-1).then_inc(consts, 1)
            for out, pattern, base in ((iota_row[:], [[1, P]], 0), (gidx[:], [[-1, GROUPS]], GROUPS),
                                       (eidx[:], [[-1, EXPERTS]], EXPERTS), (goff[:], [[TOK, GROUPS]], 0),
                                       (base_it[:], [[P, 4], [TOK, GROUPS]], 0)):
                pool.iota(out, pattern, base=base, channel_multiplier=0,
                          allow_small_or_imprecise_dtypes=True).then_inc(consts, 1)
            assert n[0] == NCHAIN

            pool.wait_ge(lb_ready, 5)
            for w in range(8):
                d, h = divmod(w, 4)
                pool.wait_ge(proj_act, EVAC[w][0])
                f = (ff, fb)[d][:, h, :]
                k = ak[:, d, h, :]
                pool.tensor_scalar(f, f, lbt[:, 3, w:w + 1], lbt[:, 2, w:w + 1], ALU.mult, ALU.add)\
                    .then_inc(gates_ready, 1)
                pool.tensor_scalar(k, k, lbt[:, 3, w:w + 1], None, ALU.mult).then_inc(gates_ready, 1)
            pool.wait_ge(gates_ready, 16)
            for lev in range(1, LEVELS + 1):
                for d, (one, tot) in enumerate(((ff, tot_f), (fb, tot_b))):
                    src = one if lev == 1 else totals(tot, lev - 1)
                    pair = src.rearrange("p h (n two) -> p h n two", two=2)
                    if lev > 1:
                        pool.wait_ge(tots_ready, 2 * (lev - 1) + d - 1)
                    pool.tensor_tensor(totals(tot, lev), pair[:, :, :, 0], pair[:, :, :, 1], ALU.mult)\
                        .then_inc(tots_ready, 1)
            for lev in range(LEVELS):
                pool.wait_ge(kc_ready, lev + 1)
                pool.wait_ge(tots_ready, 2 * LEVELS)
                if lev:
                    pool.wait_ge(k_step, 2 * lev)
                for d in range(2):
                    keys = halves(ak[:, d], lev)[:, :, :, d, :]
                    pool.tensor_tensor(keys, keys, block_total((ff, fb)[d], (tot_f, tot_b)[d], lev, 1 - d),
                                       ALU.mult).then_inc(k_step, 1)

        @block.scalar
        def _(act):
            act.dma_start(craw[:, 0, :], c_ctx.rearrange("(p j) -> p j", j=J)).then_inc(cond_landed, 16)
            act.dma_start(craw[:, 1, :], c[0].rearrange("(p j) -> p j", j=J)).then_inc(cond_landed, 16)
            for t in range(NT):
                act.dma_start(xres[:, t, :], x_tiles[t]).then_inc(x_landed[t], 16)
            act.dma_start(gmix[:], norm_mix_g[0].rearrange("(p j) -> p j", j=J)).then_inc(small_landed, 16)
            act.dma_start(bada[:], b_ada[0, 0:2 * D].rearrange("(v p j) -> p v j", v=2, j=J))\
                .then_inc(small_landed, 16)
            act.dma_start(wr[:], w_router.rearrange("(p j) e -> p j e", j=J)).then_inc(small_landed, 16)
            act.dma_start(brt[:], spread(b_router, EXPERTS)).then_inc(small_landed, 16)
            r0 = 0
            for src, rows in ((conv_a_w[0], CONV_A), (conv_b_w[0], CONV_B), (conv_b_b, 1), (ln_b_g, 1),
                              (ln_b_b, 1)):
                act.dma_start(cw[r0:r0 + rows, :], src).then_inc(rows_landed, 16)
                r0 += rows
            act.dma_start(gw[0:4, :], gnorm_c_g.rearrange("o (h v) -> (o h) v", h=HEADS)).then_inc(rows_landed, 16)
            act.dma_start(gw[4:12, :], lb_logits.rearrange("d l (h k) -> (d l h) k", h=HEADS))\
                .then_inc(rows_landed, 16)

            act.wait_ge(cond_landed, 32)
            act.activation(csig[:], craw[:], ACT.Sigmoid).then_inc(csig_ready, 1)
            for t in range(NT):
                act.wait_ge(x_landed[t], 16)
                if t:
                    act.wait_ge(ssq_ready, t)
                act.activation(junk, xres[:, t, :], ACT.Square, accum_out=ssq[:, 0, t:t + 1]).then_inc(ssq_ready, 1)
            act.wait_ge(ssq_ready, NT)
            act.wait_ge(consts, 3)
            act.activation(std[:, 0, :], ssq[:, 0, :], ACT.Sqrt, bias=eps[:], scale=1.0 / D).then_inc(std_ready, 1)
            act.wait_ge(par_ready, 3)
            act.activation(ct[:, 0, :], bank[4][:, 0:NROW], ACT.Copy).then_inc(par_evac, 1)
            act.activation(ct[:, 1, :], bank[4][:, 64:64 + NROW], ACT.Copy).then_inc(par_evac, 1)
            act.activation(gt[:], bank[4][:, 128:140], ACT.Copy).then_inc(par_evac, 1)
            act.wait_ge(lb_ready, 1)
            act.activation(lbt[:, 0, :], lbt[:, 0, :], ACT.Exp).then_inc(lb_ready, 1)

            def ada_evacuate(blk):
                a, half = divmod(blk, 2)
                slot = ADA[a][1]
                act.wait_ge(ada_used, 4 * (blk + 1))
                act.activation(part[:, slot, half * 512:(half + 1) * 512], bank[6 + blk % 2][:], ACT.Copy)\
                    .then_inc(ada_evac, 1)
                if a >= G1 and half == 1:
                    act.wait_ge(ada_evac, blk + 1)
                    act.dma_start(part[2:3, slot, :], b_ada[0:1, ADA[a][0] * D:(ADA[a][0] + 1) * D])\
                        .then_inc(bias_landed[a - G1], 16)

            ada_evacuate(0)
            ada_evacuate(1)
            for j in range(J):
                act.wait_ge(xt_ready, j + 1)
                act.activation(xnt[:, j, :], bank[j % 4][:, 0:TOK], ACT.Copy).then_inc(xt_evac, 1)
            ada_evacuate(2)
            ada_evacuate(3)

            def high(s, slot, landed, landed_at, free_at=None):
                act.wait_ge(landed, landed_at)
                if free_at is not None:
                    act.wait_ge(w_used, free_at)
                act.activation(whi[:, s, :], raw[:, slot, :], ACT.Copy).then_inc(hi_ready, 1)

            split_chunks = [(n, x) for n, x in enumerate(FRONT) if x[0] != "ada"]

            def high_front(s):
                if s < NFS:
                    n = split_chunks[s][0]
                    high(s % NSPLIT, n % NRAW, w_landed[n % NRAW], 16 * (n // NRAW + 1),
                         s - NSPLIT + 1 if s >= NSPLIT else None)

            high_front(0)
            high_front(1)
            for j in range(J):
                act.wait_ge(h_ready, 2 * j + 2)
                act.activation(lhs_hi[:, j * TOK:(j + 1) * TOK], xnt[:, j, :], ACT.Copy).then_inc(h_hi, 1)

            def assemble_keys(lev):
                if lev == 0:
                    act.wait_ge(gates_ready, 16)
                    act.wait_ge(score_ready, NT)
                    dst = ksum
                else:
                    act.wait_ge(k_step, 2 * lev)
                    act.wait_ge(q_step, 2)
                    act.wait_ge(score_ready, NT * (lev + 1))
                    dst = ff
                w = 1 << lev
                out = dst.rearrange("p h (n two w) -> p (h n) two w", two=2, w=w)
                base = ak[:, 0, 0, 0:1]
                src = bass.AP(base.tensor, base.offset, [list(base.ap[0]), [2 * w, HW // (2 * w)], [HW + w, 2],
                                                         [1, w]])
                act.activation(out, src, ACT.Copy).then_inc(kc_ready, 1)
                if lev == 1:
                    act.dma_start(s0, state_hgrn[0, 0].rearrange("d h k v -> k d h v"))\
                        .then_inc(state_landed, 16)

            def blocks_before(n):
                if n == NWIN:
                    return 12
                return sum(x[0] == "ada" for x in FRONT[:FRONT.index(("win", n))]) // 4

            blk = 4
            for n in range(NWIN):
                high_front(n + 2)
                kind, h = WIN[n]
                if kind != "i":
                    act.wait_ge(w_used, n + 1)
                    ps = bank[n % 2][:, 0:TOK]
                    if kind in ("ff", "fb"):
                        d = kind == "fb"
                        act.activation((ff, fb)[d][:, h, :], ps, ACT.Sigmoid).then_inc(proj_act, 1)
                        act.activation(ak[:, int(d), h, :], ps, ACT.Sigmoid, scale=-1.0).then_inc(proj_act, 1)
                    elif kind == "q":
                        act.activation(qh[:, h, :], ps, ACT.Sigmoid).then_inc(proj_act, 1)
                    elif kind == "bg":
                        act.activation(ub[:, h, :], ps, ACT.Sigmoid).then_inc(proj_act, 1)
                    elif kind == "g":
                        act.activation(qh[:, h, :], ps, ACT.Sigmoid).then_inc(proj_act, 1)
                    elif kind == "ac":
                        act.activation(ua[:, h, :], ps, ACT.Copy).then_inc(proj_act, 1)
                    elif kind == "ab":
                        act.activation(ab[:, h, :], ps, ACT.Copy).then_inc(proj_act, 1)
                elif h == 3:
                    act.wait_ge(w_used, n + 1)
                    for t in range(NT):
                        act.activation(v_tok[:, t, :], bank[2 + t][:], ACT.Copy).then_inc(proj_act, 1)
                done = blocks_before(n + 1)
                if 17 <= n < 17 + LEVELS:
                    assemble_keys(n - 17)
                while blk < done:
                    ada_evacuate(blk)
                    blk += 1
            for m in range(2):
                act.wait_ge(ln_centred, m + 1)
                act.activation(ub[:, m, :], yb[:, m, :], ACT.Square).then_inc(ln_sq, 1)
            act.wait_ge(kt_ready, 4)
            for k in range(4):
                act.activation(kt[:, k], bank[k][:].rearrange("p (h s) -> p h s", h=HEADS), ACT.Copy)\
                    .then_inc(kt_evac, 1)
            act.wait_ge(ln_var, 1)
            act.activation(ub[:, 0, :], bank[7][:, 0:TOK], ACT.Sqrt, bias=eps[:], scale=1.0 / 256).then_inc(ln_std, 1)
            for d, out in ((0, st_out_f), (1, st_out_b)):
                act.wait_ge(kv_ready, d + 1)
                act.activation(out, bank[d][:], ACT.Copy).then_inc(kv_out, 1)
                act.wait_ge(kv_out, d + 1)
                act.dma_start(new_state[0, 0, d].rearrange("h k v -> k h v"),
                              out.rearrange("p (h v) -> p h v", h=HEADS)).then_inc(state_stored, 16)
            high_front(NWIN + 2)

            def head_square(h):
                act.wait_ge(o_ready, h + 1)
                if h >= 2:
                    act.wait_ge(y_lo, 2 + h - 1)
                act.activation(hn[:, h % 2, :], bank[2 + h][:, 0:TOK], ACT.Square).then_inc(o_sq, 1)

            def head_std(h):
                act.wait_ge(o_sum, h + 1)
                act.activation(hn[:, h % 2, :], bank[h % 2][:, 0:TOK], ACT.Sqrt, bias=eps[:], scale=1.0 / P)\
                    .then_inc(o_std, 1)

            def y_high(k, m, src):
                act.activation(lhs_hi[:, m * TOK:(m + 1) * TOK], src, ACT.Copy).then_inc(y_hi, 1)

            for m in range(2):
                act.wait_ge(conva_step, 11 + m)
                y_high(m, m, ya[:, m, :])

            def head_high(h):
                act.wait_ge(o_norm, 3 * h + 3)
                y_high(2 + h, 4 + h, hn[:, h % 2, :])

            head_square(0)
            head_square(1)
            head_std(0)
            head_std(1)
            head_high(0)
            head_square(2)
            head_std(2)
            head_high(1)
            head_square(3)
            head_std(3)
            head_high(2)
            head_high(3)
            for m in range(2):
                act.wait_ge(ln_norm, 5)
                act.activation(ub[:, m, :], yb[:, m, :], ACT.Sigmoid).then_inc(ln_sig, 1)
            for m in range(2):
                act.wait_ge(ln_norm, 6 + m)
                y_high(6 + m, 2 + m, yb[:, m, :])

            def row_evacuate(r):
                v, cond, half = r // 4, r // 2 % 2, r % 2
                dst = {0: row_g1, 1: row_sh2, 3: row_g2}[v]
                act.wait_ge(row_ready, r + 1)
                act.activation(dst[:, cond, half * 512:(half + 1) * 512], bank[6 + r % 2][:], ACT.Copy)\
                    .then_inc(row_act, 1)

            act.wait_ge(y_lo, 1)
            act.dma_start(row_g, spread(norm_ffn_g[0], D)).then_inc(ffn_g_landed, 16)
            for r in range(4):
                row_evacuate(r)
            for k in range(8):
                s = NWIN + k
                if k:
                    high_front(s + 2)
                if k in (0, 1):
                    row_evacuate(4 + 2 * k)
                    row_evacuate(5 + 2 * k)
                if k in (4, 5):
                    row_evacuate(4 + 2 * k)
                    row_evacuate(5 + 2 * k)
            act.wait_ge(row_dve, 4)
            act.dma_start(row_g, spread(final_norm_g, D)).then_inc(final_g_landed, 16)

            for t in range(NT):
                act.wait_ge(x2_ready, 2 * (2 * t + 2))
                act.activation(h2[:, t, :], xres[:, t, :], ACT.Square, accum_out=ssq[:, 1, t:t + 1])\
                    .then_inc(ssq_ready, 1)
                act.wait_ge(ssq_ready, NT + t + 1)
                act.activation(std[:, 1, t:t + 1], ssq[:, 1, t:t + 1], ACT.Sqrt, bias=eps[:], scale=1.0 / D)\
                    .then_inc(std_ready, 1)
            for t in range(NT):
                act.wait_ge(h2_ready, 2 * t + 2)
                act.activation(lhs_hi[:, t * D:(t + 1) * D].rearrange("q (j p) -> q j p", j=J),
                               h2[:, t, :].rearrange("q (p j) -> q j p", j=J), ACT.Copy).then_inc(h2_hi, 1)
                for half in range(2):
                    act.wait_ge(h2t_ready, 2 * t + half + 1)
                    act.activation(h2t[:, 4 * half:4 * half + 4, t * P:(t + 1) * P],
                                   bank[(2 * t + half) % 6][:].rearrange("p (j t) -> p j t", j=4), ACT.Copy)\
                        .then_inc(h2t_evac, 1)
            act.wait_ge(shifted, 1)
            act.activation(rt[:, 0], rt[:, 0], ACT.Exp).then_inc(exp_ready, 1)
            for half in range(2):
                act_gather(act, 0, half)
            for half in range(2):
                act_spread(act, 0, half)
            act.wait_ge(acc_zero, 1)
            act.activation(place_t[:], acc[:, 0, 0:TOK].rearrange("p (t s) -> p t s", t=NT), ACT.Copy)\
                .then_inc(place_t_zero, 1)
            experts(act, act_group)
            act_output(act, passes(act))
            for t in range(NT):
                act.wait_ge(x3_ready, 2 * t + 2)
                act.activation(y3[:, t, :], xres[:, t, :], ACT.Square, accum_out=ssq[:, 2, t:t + 1])\
                    .then_inc(ssq_ready, 1)
                act.wait_ge(ssq_ready, 2 * NT + t + 1)
                act.activation(std[:, 2, t:t + 1], ssq[:, 2, t:t + 1], ACT.Sqrt, bias=eps[:], scale=1.0 / D)\
                    .then_inc(std_ready, 1)

        @block.tensor
        def _(pe):
            pe.wait_ge(consts, 3)
            pe.wait_ge(const_step, NCHAIN)
            pe.wait_ge(rows_landed, 16 * 7)
            pe.transpose(bank[4][:, 0:NROW], cw[0:NROW, 0:P], ident[0:NROW, 0:NROW]).then_inc(par_ready, 1)
            pe.transpose(bank[4][:, 64:64 + NROW], cw[0:NROW, P:2 * P], ident[0:NROW, 0:NROW]).then_inc(par_ready, 1)
            pe.transpose(bank[4][:, 128:140], gw[0:12, :], ident[0:12, 0:12]).then_inc(par_ready, 1)
            pe.wait_ge(csel_ready, 2)

            def ada_chunk(n, a, half, i):
                blk = 2 * a + half
                out = bank[6 + blk % 2]
                pe.wait_ge(w_landed[n % NRAW], 16 * (n // NRAW + 1))
                if i == 0 and blk >= 2:
                    pe.wait_ge(ada_evac, blk - 1)
                for jj in range(2):
                    j = 2 * i + jj
                    q = j % 4
                    last = pe.matmul(out[32 * q:32 * q + 32, :], csel[:, j, :],
                                     raw[:, n % NRAW, jj * 512:(jj + 1) * 512], start=(j < 4), stop=(j >= 4))
                last.then_inc(ada_used, 1)

            def modulation(a):
                pe.wait_ge(ada_evac, 2 * a + 2)
                if a == 0:
                    pe.wait_ge(par_evac, 3)
                for j in range(J):
                    last = pe.matmul(bank[5 - a][:, 2 * j:2 * j + 2], part[:, ADA[a][1], j::J],
                                     sel_t[:], start=True, stop=True)
                last.then_inc(mod_ready, 1)

            for n in range(8):
                ada_chunk(n, *FRONT[n][1:])
            for j in range(J):
                if j == 0:
                    pe.wait_ge(xn_ready, NT)
                if j >= 4:
                    pe.wait_ge(xt_evac, j - 3)
                for t in range(NT):
                    last = pe.transpose(bank[j % 4][:, t * P:(t + 1) * P], xn[:, t, j::J], ident[:])
                last.then_inc(xt_ready, 1)
            modulation(0)
            for n in range(8, 16):
                ada_chunk(n, *FRONT[n][1:])
            modulation(1)

            def scores(lev):
                if lev == 0:
                    pe.wait_ge(prep_ready, 12)
                    pe.wait_ge(proj_act, EVAC[15][0])
                else:
                    pe.wait_ge(kc_ready, lev)
                    if lev > 1:
                        pe.wait_ge(q_step, 2 * (lev - 1))
                w = 1 << max(lev - 1, 0)
                keys = ksum if lev <= 1 else ff
                for t in range(NT):
                    if lev:
                        pe.wait_ge(s_merged, NT * (lev - 1) + t + 1)
                    for h in range(HEADS):
                        out = bank[2 + t][:, h * P:(h + 1) * P]
                        at = slice(t * P, (t + 1) * P)
                        if lev == 0:
                            rhs = qh[:, h, at]
                        else:
                            base = aq[:, 0, h, t * P:t * P + 1]
                            rhs = bass.AP(base.tensor, base.offset,
                                          [list(base.ap[0]), [2 * w, P // (2 * w)], [HW + w, 2], [1, w]])
                            out = out.rearrange("p (n two w) -> p n two w", two=2, w=w)
                        last = pe.matmul(out, keys[:, h, at], rhs, start=True, stop=True)
                    last.then_inc(score_ready, 1)

            def wait_split(s):
                pe.wait_ge(lo_ready, s + 1)

            def win_chunk(n):
                kind, h = WIN[n]
                s = n
                slot = s % NSPLIT
                wait_split(s)
                if kind != "i":
                    m = n - 2
                    while m >= 0 and WIN[m][0] == "i":
                        m -= 2
                    if m >= 0:
                        if act_ops(WIN[m][0])[1]:
                            pe.wait_ge(proj_dve, EVAC[m][1])
                        else:
                            pe.wait_ge(proj_act, EVAC[m][0])
                    for j in range(J):
                        if n == 0:
                            pe.wait_ge(h_lo, j + 1)
                        w = slice(j * P, (j + 1) * P)
                        x = slice(j * TOK, (j + 1) * TOK)
                        last = three(pe, bank[n % 2][:, 0:TOK], whi[:, slot, w], wlo[:, slot, w],
                                     lhs_hi[:, x], lhs_lo[:, x], j == 0, j == J - 1)
                else:
                    for jj in range(2):
                        j = 2 * h + jj
                        w = slice(jj * 512, (jj + 1) * 512)
                        for t in range(NT):
                            x = slice(j * TOK + t * P, j * TOK + (t + 1) * P)
                            last = three(pe, bank[2 + t][:], lhs_hi[:, x], lhs_lo[:, x],
                                         whi[:, slot, w], wlo[:, slot, w], j == 0, j == J - 1)
                last.then_inc(w_used, 1)

            for n in range(16, NFRONT - 8):
                x = FRONT[n]
                if x[0] == "ada":
                    ada_chunk(n, *x[1:])
                else:
                    win_chunk(x[1])
                    if x[1] >= 17 and x[1] <= 17 + LEVELS:
                        scores(x[1] - 17)
            pe.wait_ge(convb_step, 2 * NTAPB)
            pe.wait_ge(ada_evac, 12)
            for m in range(2):
                last = pe.matmul(bank[6][:, 0:TOK], ones[:], yb[:, m, :], start=(m == 0), stop=(m == 1))
            last.then_inc(ln_mean, 1)
            pe.wait_ge(k_step, 2 * LEVELS)
            pe.wait_ge(s_merged, NT * (LEVELS + 1))
            pe.wait_ge(proj_act, EVAC[NWIN - 1][0])
            groups = [(0, 0), (1, 0), (0, 1), (1, 2)]
            for k, (d, t) in enumerate(groups):
                for h in range(HEADS):
                    last = pe.transpose(bank[k][:, h * P:(h + 1) * P], ak[:, d, h, t * P:(t + 1) * P], ident[:])
                last.then_inc(kt_ready, 1)
            pe.wait_ge(ln_sq, 2)
            for m in range(2):
                last = pe.matmul(bank[7][:, 0:TOK], ones[:], ub[:, m, :], start=(m == 0), stop=(m == 1))
            last.then_inc(ln_var, 1)
            for k, (d, t) in enumerate(groups):
                pe.wait_ge(kt_evac, k + 1)
                for h in range(HEADS):
                    last = pe.matmul(bank[k][:, h * P:(h + 1) * P], kt[:, k, h, :],
                                     v_tok[:, t, h * P:(h + 1) * P], start=True, stop=True)
                last.then_inc(kv_ready, 1)
            for h in range(HEADS):
                if h == 0:
                    pe.wait_ge(state_landed, 16)
                    pe.wait_ge(q_step, 2 * LEVELS)
                    pe.wait_ge(state_ready, 8)
                out = bank[2 + h]
                hs = slice(h * P, (h + 1) * P)
                for t in range(NT):
                    at = slice(t * P, (t + 1) * P)
                    last = pe.matmul(out[:, at], v_tok[:, t, hs], smat[:, t, h, :], start=True, stop=(t == 0))
                    if t:
                        before = s0[:, 0, hs] if t == 1 else sf2[:, h, :]
                        after = sb1[:, h, :] if t == 1 else s0[:, 1, hs]
                        pe.matmul(out[:, at], before, aq[:, 1, h, at], start=False, stop=False)
                        last = pe.matmul(out[:, at], after, aq[:, 0, h, at], start=False, stop=True)
                last.then_inc(o_ready, 1)

            def row(r):
                v, cond, half = r // 4, r // 2 % 2, r % 2
                slot = ADA[G1 + v][1]
                if r % 4 == 0:
                    pe.wait_ge(bias_landed[v], 16)
                if r == 0:
                    pe.wait_ge(ln_centred, 2)
                    pe.wait_ge(ln_std, 1)
                if r >= 2:
                    if (r - 2) // 4 == 2:
                        pe.wait_ge(row_dve, r - 2 - 8 + 1)
                    else:
                        pe.wait_ge(row_act, r - 2 + 1 - (4 if r - 2 >= 8 else 0))
                pe.matmul(bank[6 + r % 2][:], sel_b[:, cond, :], part[:, slot, half * 512:(half + 1) * 512],
                          start=True, stop=True).then_inc(row_ready, 1)

            for h in range(HEADS):
                pe.wait_ge(o_sq, h + 1)
                if h == 0:
                    pe.wait_ge(kv_out, 2)
                if h >= 2:
                    pe.wait_ge(o_std, h - 1)
                pe.matmul(bank[h % 2][:, 0:TOK], ones[:], hn[:, h % 2, :], start=True, stop=True)\
                    .then_inc(o_sum, 1)
            for r in range(4):
                row(r)
            for k in range(8):
                s = NWIN + k
                m = WOUT[k]
                wait_split(s)
                pe.wait_ge(y_lo, k + 1)
                if k == 0:
                    pe.wait_ge(o_norm, 12)
                for t in range(NT):
                    for half in range(2):
                        x = slice(m * TOK + t * P, m * TOK + (t + 1) * P)
                        w = slice(half * 512, (half + 1) * 512)
                        last = three(pe, bank[2 * t + half][:], lhs_hi[:, x], lhs_lo[:, x],
                                     whi[:, s % NSPLIT, w], wlo[:, s % NSPLIT, w], k == 0, k == 7)
                last.then_inc(w_used, 1)
                if k < 6:
                    row(4 + 2 * k)
                    row(5 + 2 * k)
            for t in range(NT):
                pe.wait_ge(h2_ready, 2 * t + 2)
                if t == 0:
                    pe.wait_ge(x2_ready, 4 * NT)
                for half in range(2):
                    for jj in range(4):
                        j = 4 * half + jj
                        last = pe.transpose(bank[(2 * t + half) % 6][:, jj * P:(jj + 1) * P], h2[:, t, j::J],
                                            ident[:])
                    last.then_inc(h2t_ready, 1)
            pe.wait_ge(small_landed, 64)
            pe.wait_ge(row_act, 12)
            for t in range(NT):
                pe.wait_ge(h2t_evac, 2 * t + 2)
                for j in range(J):
                    last = pe.matmul(bank[6][:, t * EXPERTS:(t + 1) * EXPERTS], h2t[:, j, t * P:(t + 1) * P],
                                     wr[:, j, :], start=(j == 0), stop=(j == J - 1))
            last.then_inc(logits_ready, 1)
            pe.wait_ge(group_ready, 1)
            pe.wait_ge(consts, 10)
            gsel = rt[:, 3, :, 0:GROUPS]
            rank = bank[7][:, 0:NT * GROUPS]
            pe.matmul(rank.rearrange("p (t g) -> p t g", g=GROUPS), upper[:], gsel, start=True, stop=False)
            for a, b in ((0, 1), (0, 2), (1, 2)):
                pe.matmul(rank[:, b * GROUPS:(b + 1) * GROUPS], ones[:], gsel[:, a, :], start=False,
                          stop=(b == 2 and a == 1))
            for t in range(NT):
                last = pe.matmul(bank[5][:, 0:GROUPS], ones[:], gsel[:, t, :], start=(t == 0), stop=(t == NT - 1))
            last.then_inc(rank_ready, 1)
            pe.wait_ge(h2_lo, NT)
            for half in range(2):
                pe_gather(pe, 0, half, first=True)
            for half in range(2):
                pe_spread(pe, 0, half, first=True)
            pe_slot_gate(pe, 0, first=True)
            pe.wait_ge(place_t_zero, 1)
            experts(pe, pe_group)
            done = passes(pe)
            for t in range(NT):
                pe_combine(pe, done, t)

        @block.vector
        def _(dve):
            n_step = [0]

            def step(ins):
                n_step[0] += 1
                ins.then_inc(vec_step, 1)
                dve.wait_ge(vec_step, n_step[0])

            step(dve.memset(csel[:], 0.0))
            dve.wait_ge(csig_ready, 1)
            for cond in range(2):
                dve.tensor_tensor(csel[:, :, cond:cond + 1].rearrange("p j o -> p (j o)"), craw[:, cond, :],
                                  csig[:, cond, :], ALU.mult).then_inc(csel_ready, 1)
            dve.wait_ge(const_step, NCHAIN)
            step(dve.tensor_tensor(int_c, int_a, int_b, ALU.bitwise_xor))
            for lev in range(LEVELS):
                dve.tensor_single_scalar(masks[:, lev, :], int_c, 1 << lev, ALU.is_ge).then_inc(masks_ready, 1)
            dve.wait_ge(std_ready, 1)
            dve.reciprocal(rstd[:, 0, :], std[:, 0, :]).then_inc(rstd_ready, 1)
            dve.wait_ge(rstd_ready, 1)
            for t in range(NT):
                dve.tensor_scalar(xn[:, t, :], xres[:, t, :], rstd[:, 0, t:t + 1], None, ALU.mult)\
                    .then_inc(xn_ready, 1)
            dve.wait_ge(par_evac, 3)
            dve.tensor_tensor(lbt[:, 0, :], gt[:, 4:12], gt[:, 4:12], ALU.subtract).then_inc(lb_ready, 1)
            dve.wait_ge(lb_ready, 2)
            step(dve.reciprocal(lbt[:, 1, :], lbt[:, 0, :]))
            dve.tensor_tensor(lbt[:, 1, :], lbt[:, 0, :], lbt[:, 1, :], ALU.mult).then_inc(lb_ready, 1)
            dve.wait_ge(lb_ready, 3)
            dve.tensor_tensor(lbt[:, 2, :], lbt[:, 1, :], lbt[:, 1, :], ALU.subtract).then_inc(lb_ready, 1)
            dve.wait_ge(lb_ready, 4)
            dve.tensor_scalar(lbt[:, 3, :], lbt[:, 2, :], -1.0, 1.0, ALU.mult, ALU.add).then_inc(lb_ready, 1)

            def per_cond(v):
                return v.rearrange("p (j o) -> p j o", o=1).broadcast_to([P, J, 2])

            dve.wait_ge(small_landed, 64)
            dve.wait_ge(mod_ready, 1)
            step(dve.tensor_tensor(scl[:], bank[5][:, 0:16].rearrange("p (j c) -> p j c", c=2),
                                   per_cond(bada[:, 1, :]), ALU.add))
            dve.scalar_tensor_tensor(out=scl[:], in0=scl[:], scalar=1.0, in1=per_cond(gmix[:]), op0=ALU.add,
                                     op1=ALU.mult).then_inc(mod_done, 1)
            dve.wait_ge(mod_ready, 2)
            dve.tensor_tensor(shf[:], bank[4][:, 0:16].rearrange("p (j c) -> p j c", c=2),
                              per_cond(bada[:, 0, :]), ALU.add).then_inc(mod_done, 1)
            dve.wait_ge(mod_done, 2)

            def low(s, slot, at):
                dve.wait_ge(hi_ready, at)
                dve.tensor_tensor(wlo[:, s, :], raw[:, slot, :], whi[:, s, :].bitcast(F32), ALU.subtract)\
                    .then_inc(lo_ready, 1)

            split_raw = [n for n, x in enumerate(FRONT) if x[0] != "ada"]

            def low_front(s):
                if s < NFS:
                    low(s % NSPLIT, split_raw[s] % NRAW, s + 1)

            def h_low(j):
                dve.wait_ge(h_hi, j + 1)
                x = slice(j * TOK, (j + 1) * TOK)
                dve.tensor_tensor(lhs_lo[:, x], xnt[:, j, :], lhs_hi[:, x].bitcast(F32), ALU.subtract)\
                    .then_inc(h_lo, 1)

            for j in range(J):
                dve.wait_ge(xt_evac, j + 1)
                for cond, cols in ((0, slice(0, CTX)), (1, slice(CTX, TOK))):
                    dve.tensor_scalar(xnt[:, j, cols], xnt[:, j, cols], scl[:, j, cond:cond + 1],
                                      shf[:, j, cond:cond + 1], ALU.mult, ALU.add).then_inc(h_ready, 1)
                if j == 1:
                    low_front(0)
                if j == 3:
                    low_front(1)
                if j:
                    h_low(j - 1)
            h_low(J - 1)

            def merge(lev):
                for t in range(NT):
                    dve.wait_ge(score_ready, NT * lev + t + 1)
                    src = bank[2 + t][:].rearrange("p (h t) -> p h t", h=HEADS)
                    if lev == 0:
                        dve.tensor_copy(smat[:, t], src).then_inc(s_merged, 1)
                    else:
                        dve.wait_ge(s_merged, NT * (lev - 1) + t + 1)
                        mask = masks[:, lev - 1:lev, :].broadcast_to([P, HEADS, P])
                        dve.copy_predicated(smat[:, t], mask, src).then_inc(s_merged, 1)

            def decay_queries(lev):
                dve.wait_ge(tots_ready, 2 * LEVELS)
                if lev:
                    dve.wait_ge(q_step, 2 * lev)
                for d in range(2):
                    x = halves(aq[:, 1 - d], lev)[:, :, :, 1 - d, :]
                    dve.tensor_tensor(x, x, block_total((ff, fb)[d], (tot_f, tot_b)[d], lev, d), ALU.mult)\
                        .then_inc(q_step, 1)

            w_a = lambda m, k: ct[:, m, k:k + 1]
            w_b = lambda m, k: ct[:, m, CONV_A + k:CONV_A + k + 1]
            extra = lambda m, k: ct[:, m, CONV_A + CONV_B + k:CONV_A + CONV_B + k + 1]
            nb = [0]

            def conv_b(first, last):
                for tap in range(first, last):
                    for m in range(2):
                        u, y = ub[:, m, :], yb[:, m, :]
                        nb[0] += 1
                        if nb[0] > 2:
                            dve.wait_ge(convb_step, nb[0] - 2)
                        if tap == 0:
                            dve.tensor_scalar(y, u, w_b(m, CONV_B // 2), extra(m, 0), ALU.mult, ALU.add)\
                                .then_inc(convb_step, 1)
                            continue
                        along, d = TAPS_B[tap]
                        if along == "time":
                            lo, hi, shift = max(0, -d), min(CTX, CTX - d), d
                        else:
                            lo, hi = CTX + max(0, -d) * GRID_W, TOK - max(0, d) * GRID_W
                            shift = d * GRID_W
                        w = w_b(m, CONV_B // 2 + d)
                        dve.scalar_tensor_tensor(out=y[:, lo:hi], in0=u[:, lo + shift:hi + shift], scalar=w,
                                                 in1=y[:, lo:hi], op0=ALU.mult, op1=ALU.add)\
                            .then_inc(convb_step, 1)

            def conv_a():
                for m in range(2):
                    dve.tensor_scalar(ya[:, m, :], ua[:, m, :], w_a(m, 1), None, ALU.mult).then_inc(conva_step, 1)
                for d in (-1, 1):
                    for m in range(2):
                        y, u = ya[:, m, :], ua[:, m, :]
                        dve.wait_ge(conva_step, 2 if d < 0 else 6)
                        rows_y = y[:, CTX:TOK].rearrange("p (r w) -> p r w", w=GRID_W)
                        rows_u = u[:, CTX:TOK].rearrange("p (r w) -> p r w", w=GRID_W)
                        lo, hi = max(0, -d), GRID_W - max(0, d)
                        dve.scalar_tensor_tensor(out=rows_y[:, :, lo:hi], in0=rows_u[:, :, lo + d:hi + d],
                                                 scalar=w_a(m, 1 + d), in1=rows_y[:, :, lo:hi], op0=ALU.mult,
                                                 op1=ALU.add).then_inc(conva_step, 1)
                        lo, hi = max(0, -d), CTX - max(0, d)
                        dve.scalar_tensor_tensor(out=y[:, lo:hi], in0=u[:, lo + d:hi + d], scalar=w_a(m, 1 + d),
                                                 in1=y[:, lo:hi], op0=ALU.mult, op1=ALU.add)\
                            .then_inc(conva_step, 1)

            for n in range(NWIN):
                low_front(n + 2)
                kind, h = WIN[n]
                ps = bank[n % 2][:, 0:TOK]
                if kind in ("q", "ba", "g", "ax"):
                    dve.wait_ge(w_used, n + 1)
                    if kind in ("q", "g"):
                        dve.wait_ge(proj_act, EVAC[n][0])
                if kind == "q":
                    dve.scalar_tensor_tensor(out=qh[:, h, :], in0=ps, scalar=float(P) ** -0.5, in1=qh[:, h, :],
                                             op0=ALU.mult, op1=ALU.mult).then_inc(proj_dve, 1)
                    dve.wait_ge(proj_dve, EVAC[n][1])
                    dve.wait_ge(gates_ready, 8 + 2 * h + 2)
                    dve.tensor_tensor(ksum[:, h, :], ak[:, 0, h, :], ak[:, 1, h, :], ALU.add).then_inc(prep_ready, 1)
                    dve.tensor_tensor(aq[:, 1, h, :], qh[:, h, :], ff[:, h, :], ALU.mult).then_inc(prep_ready, 1)
                    dve.tensor_tensor(aq[:, 0, h, :], qh[:, h, :], fb[:, h, :], ALU.mult).then_inc(prep_ready, 1)
                elif kind == "ba":
                    dve.wait_ge(proj_act, EVAC[17][0])
                    dve.tensor_tensor(ub[:, h, :], ps, ub[:, h, :], ALU.mult).then_inc(proj_dve, 1)
                elif kind == "g":
                    dve.scalar_tensor_tensor(out=qh[:, h, :], in0=ps, scalar=gt[:, h:h + 1], in1=qh[:, h, :],
                                             op0=ALU.mult, op1=ALU.mult).then_inc(proj_dve, 1)
                elif kind == "ax":
                    dve.wait_ge(proj_act, EVAC[25][0])
                    dve.tensor_tensor(ua[:, h, :], ps, ua[:, h, :], ALU.mult).then_inc(proj_dve, 1)
                if n == 17:
                    dve.wait_ge(masks_ready, LEVELS)
                    dve.wait_ge(prep_ready, 12)
                if 17 <= n <= 17 + LEVELS:
                    merge(n - 17)
                    if n > 17:
                        decay_queries(n - 18)
                if n == 19:
                    dve.wait_ge(proj_dve, EVAC[19][1])
                if n >= 19:
                    per = -(-NTAPB // (NWIN - 19))
                    conv_b(min(NTAPB, (n - 19) * per), min(NTAPB, (n - 18) * per))
                if n == 27:
                    dve.wait_ge(proj_dve, EVAC[27][1])
                    dve.wait_ge(convb_step, nb[0])
                    conv_a()
            for m in range(2):
                dve.wait_ge(ln_mean, 1)
                dve.scalar_tensor_tensor(out=yb[:, m, :], in0=bank[6][:, 0:TOK], scalar=-1.0 / 256,
                                         in1=yb[:, m, :], op0=ALU.mult, op1=ALU.add).then_inc(ln_centred, 1)
            dve.wait_ge(proj_act, EVAC[NWIN - 1][0])
            dve.wait_ge(conva_step, 10)
            for m in range(2):
                dve.tensor_tensor(ya[:, m, :], ya[:, m, :], ab[:, m, :], ALU.mult).then_inc(conva_step, 1)

            def y_low(k, m, src):
                dve.wait_ge(y_hi, k + 1)
                x = slice(m * TOK, (m + 1) * TOK)
                dve.tensor_tensor(lhs_lo[:, x], src, lhs_hi[:, x].bitcast(F32), ALU.subtract).then_inc(y_lo, 1)

            dve.wait_ge(state_landed, 16)
            for d, (tot, t, old, new) in enumerate(((tot_f, 1, s0[:, 0, :], sf2), (tot_b, 2, s0[:, 1, :], sb1))):
                dve.wait_ge(kv_ready, 3 + d)
                for h in range(HEADS):
                    dve.scalar_tensor_tensor(out=new[:, h, :], in0=old[:, h * P:(h + 1) * P],
                                             scalar=totals(tot, LEVELS)[:, h, t:t + 1],
                                             in1=bank[2 + d][:, h * P:(h + 1) * P], op0=ALU.mult, op1=ALU.add)\
                        .then_inc(state_ready, 1)
            low_front(NWIN + 2)
            for m in range(2):
                y_low(m, m, ya[:, m, :])
            for h in range(HEADS):
                o = hn[:, h % 2, :]
                dve.wait_ge(o_std, h + 1)
                dve.reciprocal(o, o).then_inc(o_norm, 1)
                dve.wait_ge(o_norm, 3 * h + 1)
                dve.tensor_tensor(o, bank[2 + h][:, 0:TOK], o, ALU.mult).then_inc(o_norm, 1)
                dve.wait_ge(o_norm, 3 * h + 2)
                dve.tensor_tensor(o, o, qh[:, h, :], ALU.mult).then_inc(o_norm, 1)
                if h:
                    y_low(1 + h, 3 + h, hn[:, (h - 1) % 2, :])
            y_low(5, 7, hn[:, 1, :])
            dve.wait_ge(ln_std, 1)
            dve.reciprocal(ub[:, 0, :], ub[:, 0, :]).then_inc(ln_norm, 1)
            for m in range(2):
                dve.wait_ge(ln_norm, 1 + 2 * m)
                dve.tensor_tensor(yb[:, m, :], yb[:, m, :], ub[:, 0, :], ALU.mult).then_inc(ln_norm, 1)
                dve.wait_ge(ln_norm, 2 + 2 * m)
                dve.tensor_scalar(yb[:, m, :], yb[:, m, :], extra(m, 1), extra(m, 2), ALU.mult, ALU.add)\
                    .then_inc(ln_norm, 1)
            for m in range(2):
                dve.wait_ge(ln_sig, 2)
                dve.tensor_tensor(yb[:, m, :], yb[:, m, :], ub[:, m, :], ALU.mult).then_inc(ln_norm, 1)
            for m in range(2):
                y_low(6 + m, 2 + m, yb[:, m, :])
            for k in range(8):
                if k:
                    low_front(NWIN + k + 2)
                if k in (2, 3):
                    dve.wait_ge(ffn_g_landed, 16)
                    for r in (4 + 2 * k, 5 + 2 * k):
                        cond, half = r // 2 % 2, r % 2
                        cols = slice(half * 512, (half + 1) * 512)
                        dve.wait_ge(row_ready, r + 1)
                        dve.scalar_tensor_tensor(out=row_sc2[:, cond, cols], in0=bank[6 + r % 2][:], scalar=1.0,
                                                 in1=row_g[:, cols], op0=ALU.add, op1=ALU.mult)\
                            .then_inc(row_dve, 1)
            dve.wait_ge(w_used, NWIN + 8)
            dve.wait_ge(row_act, 4)
            for t in range(NT):
                for half in range(2):
                    o = 2 * t + half
                    cols = slice(half * 512, (half + 1) * 512)
                    gated = h2[:, t, cols]
                    dve.tensor_tensor(gated, bank[o][:], row_g1[:, COND[t], cols], ALU.mult).then_inc(x2_ready, 1)
                    dve.wait_ge(x2_ready, 2 * o + 1)
                    dve.tensor_tensor(xres[:, t, cols], xres[:, t, cols], gated, ALU.add).then_inc(x2_ready, 1)
            dve.wait_ge(row_dve, 4)
            dve.wait_ge(row_act, 8)
            for t in range(NT):
                dve.wait_ge(std_ready, 2 + t)
                dve.reciprocal(rstd[:, 1, t:t + 1], std[:, 1, t:t + 1]).then_inc(rstd_ready, 1)
                dve.wait_ge(rstd_ready, 2 + t)
                dve.scalar_tensor_tensor(out=h2[:, t, :], in0=xres[:, t, :], scalar=rstd[:, 1, t:t + 1],
                                         in1=row_sc2[:, COND[t], :], op0=ALU.mult, op1=ALU.mult)\
                    .then_inc(h2_ready, 1)
                dve.wait_ge(h2_ready, 2 * t + 1)
                dve.tensor_tensor(h2[:, t, :], h2[:, t, :], row_sh2[:, COND[t], :], ALU.add).then_inc(h2_ready, 1)
            for t in range(NT):
                dve.wait_ge(h2_hi, t + 1)
                x = slice(t * D, (t + 1) * D)
                dve.tensor_tensor(lhs_lo[:, x].rearrange("q (j p) -> q j p", j=J),
                                  h2[:, t, :].rearrange("q (p j) -> q j p", j=J),
                                  lhs_hi[:, x].bitcast(F32).rearrange("q (j p) -> q j p", j=J), ALU.subtract)\
                    .then_inc(h2_lo, 1)

            def r3(k, n=EXPERTS):
                return rt[:, k, :, 0:n]

            def one(k):
                return rt[:, k, :, 0:1]

            def bc(k, n):
                return one(k).broadcast_to([P, NT, n])

            def table(t, n):
                return t[:].rearrange("p (o n) -> p o n", o=1).broadcast_to([P, NT, n])

            logits = bank[6][:, 0:NT * EXPERTS].rearrange("p (t e) -> p t e", e=EXPERTS)
            dve.wait_ge(logits_ready, 1)
            step(dve.tensor_reduce(one(1), logits, AX, ALU.max))
            dve.tensor_tensor(r3(0), logits, bc(1, EXPERTS), ALU.subtract).then_inc(shifted, 1)
            dve.wait_ge(exp_ready, 1)
            step(dve.tensor_reduce(one(1), r3(0), AX, ALU.add))
            step(dve.reciprocal(one(1), one(1)))
            step(dve.tensor_tensor(r3(0), r3(0), bc(1, EXPERTS), ALU.mult))
            step(dve.tensor_tensor(r3(2), r3(0), table(brt, EXPERTS), ALU.add))
            v = rt[:, 2].rearrange("p t (g e) -> p (t g) e", g=GROUPS)
            at = 0
            for far in (1, 2, 3):
                m = PER_GROUP - far
                ins = dve.tensor_tensor(rpair[:, :, at:at + m], v[:, :, 0:m], v[:, :, far:PER_GROUP], ALU.add)
                at += m
                n_step[0] += 1
                ins.then_inc(vec_step, 1)
            dve.wait_ge(vec_step, n_step[0])
            gs = rt[:, 4].rearrange("p t e -> p (t e)")[:, 0:NT * GROUPS]
            gs3 = gs.rearrange("p (t g) -> p t g", g=GROUPS)
            step(dve.tensor_reduce(gs.rearrange("p (a o) -> p a o", o=1), rpair[:], AX, ALU.max))

            def first_max(out, values, scratch, m, order, n):
                step(dve.tensor_reduce(one(m), values, AX, ALU.max))
                step(dve.tensor_tensor(scratch, values, bc(m, n), ALU.is_equal))
                step(dve.tensor_tensor(scratch, scratch, table(order, n), ALU.mult))
                step(dve.tensor_reduce(one(m), scratch, AX, ALU.max))
                return dve.tensor_tensor(out, scratch, bc(m, n), ALU.is_equal)

            first_max(r3(3, GROUPS), gs3, r3(5, GROUPS), 1, gidx, GROUPS).then_inc(group_ready, 1)
            dve.wait_ge(group_ready, 1)
            ing = rt[:, 3, :, 0:GROUPS].rearrange("p t (g o) -> p t g o", o=1)\
                .broadcast_to([P, NT, GROUPS, PER_GROUP])
            four = lambda k: rt[:, k].rearrange("p t (g e) -> p t g e", g=GROUPS)
            step(dve.tensor_tensor(four(6), four(2), ing, ALU.mult))
            step(dve.tensor_scalar(r3(7, GROUPS), r3(3, GROUPS), 1e9, -1e9, ALU.mult, ALU.add))
            out_of = rt[:, 7, :, 0:GROUPS].rearrange("p t (g o) -> p t g o", o=1)\
                .broadcast_to([P, NT, GROUPS, PER_GROUP])
            step(dve.tensor_tensor(four(6), four(6), out_of, ALU.add))
            step(first_max(r3(8), r3(6), r3(5), 1, eidx, EXPERTS))
            step(dve.scalar_tensor_tensor(out=r3(6), in0=r3(8), scalar=-3e9, in1=r3(6), op0=ALU.mult, op1=ALU.add))
            step(first_max(r3(9), r3(6), r3(5), 1, eidx, EXPERTS))
            step(dve.tensor_tensor(r3(8), r3(8), r3(9), ALU.add))
            step(dve.tensor_tensor(r3(8), r3(8), r3(0), ALU.mult))
            step(dve.tensor_reduce(one(1), r3(8), AX, ALU.add))
            step(dve.reciprocal(one(1), one(1)))
            step(dve.tensor_tensor(gates[:, :, 0:EXPERTS], r3(8), bc(1, EXPERTS), ALU.mult))
            step(dve.tensor_copy(gates[:, :, EXPERTS:], gates[:, :, 0:PER_GROUP]))
            dve.wait_ge(rank_ready, 1)
            rank = bank[7][:, 0:NT * GROUPS].rearrange("p (t g) -> p t g", g=GROUPS)
            step(dve.tensor_tensor(r3(10, GROUPS), rank, table(goff, GROUPS), ALU.add))
            step(dve.tensor_tensor(r3(10, GROUPS), r3(10, GROUPS), r3(3, GROUPS), ALU.mult))
            step(dve.tensor_reduce(code[:].rearrange("p (t o) -> p t o", o=1), r3(10, GROUPS), AX, ALU.add))
            step(dve.tensor_tensor(codem[:], code[:].rearrange("p (t o) -> p t o", o=1)
                                   .broadcast_to([P, NT, 4 * GROUPS]),
                                   base_it[:].rearrange("p (o n) -> p o n", o=1).broadcast_to([P, NT, 4 * GROUPS]),
                                   ALU.subtract))
            step(dve.tensor_reduce(flagf[:], bank[5][:, 0:GROUPS], AX, ALU.max))
            dve.tensor_scalar(flag[:], flagf[:], float(P), None, ALU.is_gt).then_inc(flag_ready, 1)
            vec_place(dve, 0, 0)
            for half in range(2):
                vec_spread(dve, 0, half)
            dve.memset(acc[:], 0.0).then_inc(acc_zero, 1)
            vec_slot_gate(dve, 0)
            dve.wait_ge(acc_zero, 1)
            experts(dve, vec_group)
            done = passes(dve)
            vec_output(dve, done)
            for t in range(NT):
                vec_combine(dve, done, t)
            dve.wait_ge(comb_added, done * 6 + 6)
            dve.wait_ge(row_act, 12)
            dve.wait_ge(final_g_landed, 16)
            for t in range(NT):
                dve.tensor_tensor(acc[:, t, :], acc[:, t, :], row_g2[:, COND[t], :], ALU.mult).then_inc(x3_ready, 1)
                dve.wait_ge(x3_ready, 2 * t + 1)
                dve.tensor_tensor(xres[:, t, :], xres[:, t, :], acc[:, t, :], ALU.add).then_inc(x3_ready, 1)
            for t in range(NT):
                dve.wait_ge(std_ready, 1 + NT + t + 1)
                dve.reciprocal(rstd[:, 2, t:t + 1], std[:, 2, t:t + 1]).then_inc(rstd_ready, 1)
                dve.wait_ge(rstd_ready, 1 + NT + t + 1)
                dve.scalar_tensor_tensor(out=y3[:, t, :], in0=xres[:, t, :], scalar=rstd[:, 2, t:t + 1],
                                         in1=row_g, op0=ALU.mult, op1=ALU.mult).then_inc(y_ready, 1)

_INS = ["x_prompt", "x_sample", "state_hgrn", "c", "c_ctx", "norm_mix_g", "norm_ffn_g", "final_norm_g", "w_ada",
        "b_ada", "w_in", "w_out", "conv_a_w", "conv_b_w", "conv_b_b", "ln_b_g", "ln_b_b", "lb_logits",
        "gnorm_c_g", "w_router", "b_router", "w_gate", "w_up", "w_down"]
_OUTS = [(1, CTX, D), (1, LAT, D), (1, 1, 2, HEADS, P, P)]


def kernel(**inputs):
    import numpy as _np
    import concourse.bacc as _bacc
    from concourse.bass_utils import run_bass_kernel_spmd as _run

    nc = _bacc.Bacc("TRN2", target_bir_lowering=False, num_devices=1)
    arrays, args = {}, []
    for name in _INS:
        a = _np.ascontiguousarray(inputs[name])
        arrays[f"in_{name}"] = a
        args.append(nc.dram_tensor(f"in_{name}", a.shape, mybir.dt.from_np(a.dtype), kind="ExternalInput").ap())
    for i, shape in enumerate(_OUTS):
        args.append(nc.dram_tensor(f"out_{i}", shape, F32, kind="ExternalOutput").ap())
    build(nc, *args)
    r = _run(nc, [arrays], core_ids=[0])
    return tuple(r.results[0][f"out_{i}"] for i in range(len(_OUTS)))
```

```python
from contextlib import ExitStack

import concourse.bass as bass
from concourse import mybir

F32 = mybir.dt.float32
F32R = mybir.dt.float32r
I32 = mybir.dt.int32
U8 = mybir.dt.uint8
ALU = mybir.AluOpType
ACT = mybir.ActivationFunctionType
AX = mybir.AxisListType.X

P = 128
D = 1024
J = D // P
CTX, LAT, GRID_W = 128, 256, 64
TOK = CTX + LAT
NT = TOK // P
COND = [0, 1, 1]
HEADS = 4
HW = HEADS * TOK
CONV_A, CONV_B = 3, 31
NROW = CONV_A + CONV_B + 3
LEVELS = 7
EXPERTS, GROUPS, PER_GROUP = 16, 4, 4
FE = 512
EPS = 1e-6
TAPS_B = [("middle", 0)] + [("time", d) for d in range(-15, 16) if d] + [("column", r) for r in range(-3, 4) if r]
NTAPB = len(TAPS_B)
NCHAIN = 23
CHUNK = 1024

NRAW = 8
NSPLIT = 4

COL = dict(ab=0, ac=256, ax=512, ba=768, bg=1024, q=1280, i=1792, ff=2304, fb=2816, g=3328)
WIN = ([("ff", h) for h in range(4)] + [("fb", h) for h in range(4)] + [("q", h) for h in range(4)]
       + [("i", h) for h in range(4)] + [("bg", 0), ("bg", 1), ("ba", 0), ("ba", 1)]
       + [("g", h) for h in range(4)] + [("ac", 0), ("ac", 1), ("ax", 0), ("ax", 1), ("ab", 0), ("ab", 1)])
NWIN = len(WIN)
X3_AHEAD = 2
ROUTER_BANK = [6, 0, 2]
OUT_TAIL = 4
ROWS = [0, 1, 2, 3, 8, 9, 10, 11, 4, 5, 6, 7, 12, 13, 14, 15]
WOUT = [0, 1, 4, 5, 6, 7, 2, 3]
SC1, SH1, G1, SH2, SC2, G2 = range(6)
ADA = [(1, 0), (0, 1), (2, 2), (3, 3), (4, 0), (5, 1)]


def front_chunks():
    ada = [("ada", a, half, i) for a in range(6) for half in range(2) for i in range(4)]
    out, ada = ada[:16], ada[16:]
    for n in range(NWIN):
        out.append(("win", n))
        take = 2 if n < 6 or (n < 26 and n % 2 == 0) else 0
        out, ada = out + ada[:take], ada[take:]
    assert not ada
    return out + [("wout", k) for k in range(8)]


FRONT = front_chunks()
SPLIT_OF = {c: n for n, c in enumerate(x for x in FRONT if x[0] != "ada")}
NFRONT, NFS = len(FRONT), len(SPLIT_OF)
STAGES = [("G", 0), ("U", 0), ("G", 1), ("U", 1), ("D", 0), ("G", 2), ("U", 2), ("D", 1), ("G", 3), ("U", 3),
          ("D", 2), ("D", 3)]
NG = 4 * len(STAGES)
AHEAD = NSPLIT - 1

COMBINE_AFTER = [3, 9, 18]
TURN_AFTER = 25
PLACE_AT = 27
GATHER_AFTER = [30, 34]
SPREAD_AFTER = [42, 44]
SLOT_GATE_AFTER = 45


def stage_end(what, e):
    return 4 * STAGES.index((what, e)) + 4


AT_AFTER = [4 * STAGES.index(("D", e)) - (3 if e else 5) for e in range(PER_GROUP)]
assert NG % NRAW == 0 and NG % NSPLIT == 0
assert all(x[0] != "ada" for x in FRONT[-NRAW:])


def act_ops(kind):
    return {"ff": (2, 0), "fb": (2, 0), "q": (1, 1), "bg": (1, 0), "ba": (0, 1), "g": (1, 1),
            "ac": (1, 0), "ax": (0, 1), "ab": (1, 0)}[kind]


def evac_counts():
    a = d = 0
    out = []
    for kind, h in WIN:
        if kind == "i":
            a += 3 if h == 3 else 0
        else:
            x, y = act_ops(kind)
            a, d = a + x, d + y
        out.append((a, d))
    return out


EVAC = evac_counts()


def build(nc, x_prompt, x_sample, state_hgrn, c, c_ctx, norm_mix_g, norm_ffn_g, final_norm_g, w_ada, b_ada,
          w_in, w_out, conv_a_w, conv_b_w, conv_b_b, ln_b_g, ln_b_b, lb_logits, gnorm_c_g, w_router,
          b_router, w_gate, w_up, w_down, y_prompt, y_sample, new_state):
    ctx = ExitStack()
    with ctx:
        def sb(name, shape, dt=F32):
            return ctx.enter_context(nc.sbuf_tensor(name, shape, dt))

        def sem(name):
            return ctx.enter_context(nc.semaphore(name))

        raw = sb("raw", [P, NRAW, CHUNK])
        whi = sb("whi", [P, NSPLIT, CHUNK], F32R)
        wlo = sb("wlo", [P, NSPLIT, CHUNK], F32R)
        lhs_hi = sb("lhs_hi", [P, 8 * TOK], F32R)
        lhs_lo = sb("lhs_lo", [P, 8 * TOK], F32R)
        xres = sb("xres", [P, NT, D])
        part = sb("part", [P, 4, D])
        ident = sb("ident", [P, P])
        ones = sb("ones", [P, P])
        sel_t = sb("sel_t", [P, 2])
        sel_b = sb("sel_b", [P, 2, P])
        upper = sb("upper", [P, P])
        iota_row = sb("iota_row", [P, P])
        masks = sb("masks", [P, LEVELS, P], U8)
        csel = sb("csel", [P, J, 32])
        craw = sb("craw", [P, 2, J])
        csig = sb("csig", [P, 2, J])
        gmix = sb("gmix", [P, J])
        bada = sb("bada", [P, 2, J])
        scl = sb("scl", [P, J, 2])
        shf = sb("shf", [P, J, 2])
        ct = sb("ct", [P, 2, NROW])
        gt = sb("gt", [P, 12])
        lbt = sb("lbt", [P, 4, 8])
        eps = sb("eps", [P, 1])
        ssq = sb("ssq", [P, 3, NT])
        std = sb("std", [P, 3, NT])
        rstd = sb("rstd", [P, 3, NT])
        wr = sb("wr", [P, J, 32])
        sel_h = sb("sel_h", [P, HEADS, HEADS])
        sel_e = sb("sel_e", [P, EXPERTS])
        brt = sb("brt", [P, EXPERTS])
        gidx = sb("gidx", [P, GROUPS])
        eidx = sb("eidx", [P, EXPERTS])
        goff = sb("goff", [P, GROUPS])
        base_it = sb("base_it", [P, 4 * GROUPS])
        flag = sb("flag", [P, 1], I32)
        flagf = sb("flagf", [P, 1])

        FIRST, SECOND = 36 * 256, 45 * 256
        with ExitStack() as front:
            area1 = front.enter_context(nc.sbuf_tensor("front1", [P, FIRST], F32))
            area2 = front.enter_context(nc.sbuf_tensor("front2", [P, SECOND], F32))
        with ExitStack() as chain:
            rows = chain.enter_context(nc.sbuf_tensor("rows", [P, 6 * D], F32))
        ys_h = sb("ys_h", [P, D], F32R)
        ys_l = sb("ys_l", [P, D], F32R)
        at_hi = sb("at_hi", [P, 2, 4, P], F32R)
        at_lo = sb("at_lo", [P, 2, 4, P], F32R)
        hgf = sb("hgf", [P, D])
        area3 = sb("back1", [P, FIRST - 5 * D])
        hg_hi = sb("hg_hi", [P, J, P], F32R)
        hg_lo = sb("hg_lo", [P, J, P], F32R)
        place = sb("place", [P, NT, P], F32R)
        place_t = sb("place_t", [P, NT, P], F32R)
        area4 = sb("back2", [P, SECOND - (2 * J + 6) * P])

        def cut(area, at, *shape):
            n = 1
            for s in shape:
                n *= s
            v = area[:, at:at + n]
            if len(shape) == 2:
                return v.rearrange("p (a b) -> p a b", b=shape[1])
            if len(shape) == 3:
                return v.rearrange("p (a b c) -> p a b c", b=shape[1], c=shape[2])
            return v

        aq = cut(area1, 0, 2, HEADS, TOK)
        v_tok = cut(area1, 2 * HW, NT, HEADS * P)
        smat = cut(area1, 2 * HW + NT * 512, NT, HEADS, P)
        tot_f = cut(area1, 2 * HW + NT * 1024, HEADS, TOK)
        tot_b = cut(area1, 3 * HW + NT * 1024, HEADS, TOK)
        ak = cut(area2, 0, 2, HEADS, TOK)
        ff = cut(area2, 2 * HW, HEADS, TOK)
        fb = cut(area2, 3 * HW, HEADS, TOK)
        qh = cut(area2, 4 * HW, HEADS, TOK)
        ksum = cut(area2, 5 * HW, HEADS, TOK)
        ya = cut(area2, 5 * HW, 2, TOK)
        yb = cut(area2, 5 * HW + 2 * TOK, 2, TOK)
        ua = cut(area2, 6 * HW, 2, TOK)
        ab = cut(area2, 6 * HW + 2 * TOK, 2, TOK)
        ub = cut(area2, 6 * HW + 4 * TOK, 2, TOK)
        assert 6 * HW + 6 * TOK <= SECOND
        kt = cut(area2, 0, 4, HEADS, P)
        hn = cut(area2, 0, HEADS, TOK)
        hr = hn[0:HEADS, 0, :]
        og = cut(area2, HW, HEADS, TOK)
        s0 = cut(area2, 3 * HW, 2, HEADS * P)
        st_out_f = area2[:, 3 * HW + 1024:3 * HW + 1536]
        sf2 = cut(area2, 2 * HW, HEADS, P)
        sb1 = cut(area2, 2 * HW + 512, HEADS, P)
        st_out_b = area2[:, 2 * HW + 1024:2 * HW + 1536]
        xnt = cut(area2, 0, J, TOK)
        xn = cut(area1, 0, NT, D)
        junk = area1[:, NT * D:NT * D + D]
        int_a = area1[:, 5 * D:5 * D + P].bitcast(I32)
        int_b = area1[:, 5 * D + P:5 * D + 2 * P].bitcast(I32)
        int_c = area1[:, 5 * D + 2 * P:5 * D + 3 * P].bitcast(I32)
        cw = area1[:, 6 * D:6 * D + 256]
        gw = area1[:, 6 * D + 256:6 * D + 384]

        row_g1 = cut(rows, 0, 2, D)
        row_sh2 = cut(rows, 2 * D, 2, D)
        row_sc2 = cut(rows, 4 * D, 2, D)
        row_g2 = cut(area3, D, 2, D)
        row_g = area3[:, 3 * D:4 * D]
        h2 = cut(area4, 0, NT, D)
        h2t = cut(area4, NT * D, J, TOK)
        acc = cut(area4, NT * D, NT, D)
        sgate = area4[:, 0:FE]
        eact = area4[:, FE:2 * FE]
        y3 = cut(area4, 0, NT, D)
        rt = area4[:, 2 * NT * D:2 * NT * D + 11 * NT * EXPERTS]\
            .rearrange("p (k t e) -> p k t e", t=NT, e=EXPERTS)
        rpair = sb("rpair", [P, NT * GROUPS, 6])
        code = sb("code", [P, NT])
        codem = sb("codem", [P, NT, 4 * GROUPS])
        gates = sb("gates", [P, NT, EXPERTS + PER_GROUP])
        gsel4 = sb("gsel4", [P, NT, PER_GROUP])
        gate4 = sb("gate4", [P, PER_GROUP])

        bank = [ctx.enter_context(nc.psum_tensor(f"bank{i}", [P, 512], F32)) for i in range(8)]

        x_landed = [sem(f"x_landed{t}") for t in range(NT)]
        cond_landed, small_landed, rows_landed = sem("cond_landed"), sem("small_landed"), sem("rows_landed")
        w_landed = [sem(f"w_landed{i}") for i in range(NRAW)]
        state_landed, ffn_g_landed, final_g_landed = sem("state_landed"), sem("ffn_g_landed"), sem("final_g_landed")
        bias_landed = [sem(f"bias_landed{i}") for i in range(4)]
        state_stored, y_stored = sem("state_stored"), sem("y_stored")
        consts, const_step, masks_ready = sem("consts"), sem("const_step"), sem("masks_ready")
        vec_step = sem("vec_step")
        hi_ready, lo_ready, w_used = sem("hi_ready"), sem("lo_ready"), sem("w_used")
        ada_used, ada_evac, mod_ready, mod_done = sem("ada_used"), sem("ada_evac"), sem("mod_ready"), sem("mod_done")
        csig_ready, csel_ready = sem("csig_ready"), sem("csel_ready")
        std_ready, rstd_ready, xn_ready = sem("std_ready"), sem("rstd_ready"), sem("xn_ready")
        ssq_ready = sem("ssq_ready")
        par_ready, par_evac, lb_ready = sem("par_ready"), sem("par_evac"), sem("lb_ready")
        xt_ready, xt_evac = sem("xt_ready"), sem("xt_evac")
        h_ready, h_ready_pool, h_hi, h_lo = sem("h_ready"), sem("h_ready_pool"), sem("h_hi"), sem("h_lo")
        proj_act, proj_dve = sem("proj_act"), sem("proj_dve")
        gates_ready, tots_ready, prep_ready = sem("gates_ready"), sem("tots_ready"), sem("prep_ready")
        kc_ready, score_ready, s_merged = sem("kc_ready"), sem("score_ready"), sem("s_merged")
        q_step, k_step = sem("q_step"), sem("k_step")
        kt_ready, kt_evac, kv_ready, kv_out, state_ready = (sem("kt_ready"), sem("kt_evac"), sem("kv_ready"),
                                                            sem("kv_out"), sem("state_ready"))
        convb_step, conva_step = sem("convb_step"), sem("conva_step")
        ln_mean, ln_centred, ln_sq, ln_var, ln_std, ln_norm, ln_sig = (
            sem("ln_mean"), sem("ln_centred"), sem("ln_sq"), sem("ln_var"), sem("ln_std"), sem("ln_norm"),
            sem("ln_sig"))
        o_ready, o_sq, o_gated, o_sum = sem("o_ready"), sem("o_sq"), sem("o_gated"), sem("o_sum")
        o_std, o_rstd, o_spread, o_norm = sem("o_std"), sem("o_rstd"), sem("o_spread"), sem("o_norm")
        tile_done = sem("tile_done")
        y_hi, y_lo = sem("y_hi"), sem("y_lo")
        row_ready, row_act, row_dve = sem("row_ready"), sem("row_act"), sem("row_dve")
        x2_ready, h2_ready, h2t_ready, h2t_evac = sem("x2_ready"), sem("h2_ready"), sem("h2t_ready"), sem("h2t_evac")
        h2_hi, h2_lo = sem("h2_hi"), sem("h2_lo")
        logits_ready, shifted, exp_ready = sem("logits_ready"), sem("shifted"), sem("exp_ready")
        wr_zero, router_done, router_evac = sem("wr_zero"), sem("router_done"), sem("router_evac")
        group_ready, rank_ready, flag_ready = sem("group_ready"), sem("rank_ready"), sem("flag_ready")
        place_ready, gsel_ready = sem("place_ready"), sem("gsel_ready")
        gather_ready, gather_evac = sem("gather_ready"), sem("gather_evac")
        spread_ready, hg_hi_ready, hg_lo_ready = sem("spread_ready"), sem("hg_hi_ready"), sem("hg_lo_ready")
        slot_gate, slot_gate_evac, turn_ready, turn_evac = (sem("slot_gate"), sem("slot_gate_evac"),
                                                            sem("turn_ready"), sem("turn_evac"))
        silu_ready, eact_ready, at_ready, at_hi_ready, at_lo_ready = (
            sem("silu_ready"), sem("eact_ready"), sem("at_ready"), sem("at_hi_ready"), sem("at_lo_ready"))
        ys_hi, ys_lo, comb_ready, comb_added = sem("ys_hi"), sem("ys_lo"), sem("comb_ready"), sem("comb_added")
        acc_zero, place_t_zero = sem("acc_zero"), sem("place_t_zero")
        x3_ready, y_ready = sem("x3_ready"), sem("y_ready")

        ada_v = w_ada[0].rearrange("(p j) n -> p j n", j=J)
        win_v = w_in[0].rearrange("(p j) n -> p j n", j=J)
        x_tiles = [x_prompt[0], x_sample[0, 0:P, :], x_sample[0, P:2 * P, :]]
        y_tiles = [y_prompt[0], y_sample[0, 0:P, :], y_sample[0, P:2 * P, :]]

        def spread(vec, n):
            return bass.AP(vec.tensor, vec.offset, [[0, P], [1, n]])

        def front_source(x):
            if x[0] == "ada":
                _, a, half, i = x
                n0 = ADA[a][0] * D + half * 512
                return ada_v[:, 2 * i:2 * i + 2, n0:n0 + 512], 512
            if x[0] == "win":
                kind, h = WIN[x[1]]
                if kind == "i":
                    return win_v[:, 2 * h:2 * h + 2, COL["i"]:COL["i"] + 512], 512
                n0 = COL[kind] + h * P
                return win_v[:, :, n0:n0 + P], P
            m = WOUT[x[1]]
            return w_out[0, m * P:(m + 1) * P, :].rearrange("p (a n) -> p a n", a=1), CHUNK

        def raw_as(slot, inner):
            return raw[:, slot, :].rearrange("p (a n) -> p a n", n=inner)

        def raw_slot(local):
            return (NFRONT + local) % NRAW

        def split_slot(local):
            return (NFS + local) % NSPLIT

        def load_small_rows(sp):
            r0 = 0
            for src, rows in ((conv_a_w[0], CONV_A), (conv_b_w[0], CONV_B), (conv_b_b, 1), (ln_b_g, 1),
                              (ln_b_b, 1)):
                sp.dma_start(cw[r0:r0 + rows, :], src).then_inc(rows_landed, 16)
                r0 += rows
            sp.dma_start(gw[0:4, :], gnorm_c_g.rearrange("o (h v) -> (o h) v", h=HEADS)).then_inc(rows_landed, 16)
            sp.dma_start(gw[4:12, :], lb_logits.rearrange("d l (h k) -> (d l h) k", h=HEADS))\
                .then_inc(rows_landed, 16)

        def load_front(sp):
            for n, x in enumerate(FRONT):
                if n == 4:
                    load_small_rows(sp)
                if n >= NRAW:
                    old = FRONT[n - NRAW]
                    if old[0] == "ada":
                        sp.wait_ge(ada_used, sum(y[0] == "ada" for y in FRONT[:n - NRAW + 1]))
                    else:
                        sp.wait_ge(lo_ready, SPLIT_OF[old] + 1)
                src, inner = front_source(x)
                sp.dma_start(raw_as(n % NRAW, inner), src).then_inc(w_landed[n % NRAW], 16)

        def load_group(sp, it, g):
            for k, (what, e) in enumerate(STAGES):
                for i in range(4):
                    n = 4 * k + i
                    sp.wait_ge(lo_ready, it * NG + (NFS + n - NRAW + 1))
                    src = {"G": w_gate, "U": w_up, "D": w_down}[what][0, bass.ds(g * PER_GROUP + e, 1)]
                    if what == "D":
                        src = src.rearrange("o (p j) d -> (o p) j d", j=4)[:, i:i + 1, :]
                        dst = raw_as(raw_slot(n), CHUNK)
                    else:
                        src = src.rearrange("o (p j) f -> (o p) j f", j=J)[:, 2 * i:2 * i + 2, :]
                        dst = raw_as(raw_slot(n), FE)
                    sp.dma_start(dst, src).then_inc(w_landed[raw_slot(n)], 16)

        def overflow(eng):
            eng.wait_ge(flag_ready, 1)
            return eng.value_load(flag[0:1, 0:1], min_val=0, max_val=1) > 0

        def experts(eng, one_group):
            with eng.Fori(0, GROUPS) as g:
                one_group(eng, g, g)
            with eng.If(overflow(eng)):
                with eng.Fori(1, 3) as turn:
                    with eng.Fori(0, GROUPS) as g:
                        one_group(eng, turn * GROUPS + g, g)

        def passes(eng):
            eng.wait_ge(flag_ready, 1)
            return eng.value_load(flag[0:1, 0:1], min_val=0, max_val=1) * (2 * GROUPS) + GROUPS

        def totals(tot, lev):
            n = TOK >> lev
            return tot[:, :, TOK - 2 * n:TOK - n]

        def halves(a, lev):
            return a.rearrange("p h (n two w) -> p h n two w", two=2, w=1 << lev)

        def block_total(one, tot, lev, half):
            src = one if lev == 0 else totals(tot, lev)
            v = src.rearrange("p h (n two) -> p h n two", two=2)[:, :, :, half]
            n = TOK >> (lev + 1)
            return v.rearrange("p h (n o) -> p h n o", o=1).broadcast_to([P, HEADS, n, 1 << lev])

        def three(pe, out, a_hi, a_lo, b_hi, b_lo, first, last):
            pe.matmul(out, a_hi, b_hi, start=first, stop=False)
            pe.matmul(out, a_hi, b_lo, start=False, stop=False)
            return pe.matmul(out, a_lo, b_hi, start=False, stop=last)

        def vec_place(dve, it):
            for t in range(NT):
                dve.tensor_scalar(place[:, t, :], iota_row[:], codem[:, t, bass.ds(it, 1)], None, ALU.is_equal)\
                    .then_inc(place_ready, 1)

        def vec_gates(dve, g):
            dve.tensor_copy(gsel4[:], gates[:, :, bass.ds(g * PER_GROUP, PER_GROUP)]).then_inc(gsel_ready, 1)

        def pe_gather(pe, it, half, first=False):
            if half == 0:
                pe.wait_ge(place_ready, it * NT + NT)
                if not first:
                    pe.wait_ge(turn_evac, it)
            for t in range(NT):
                x = slice(t * D + half * 512, t * D + (half + 1) * 512)
                pe.matmul(bank[6 + half][:], place[:, t, :], lhs_hi[:, x], start=(t == 0), stop=False)
                last = pe.matmul(bank[6 + half][:], place[:, t, :], lhs_lo[:, x], start=False, stop=(t == NT - 1))
            last.then_inc(gather_ready, 1)

        def act_gather(act, it, half):
            act.wait_ge(gather_ready, it * 2 + (half + 1))
            act.activation(hgf[:, half * 512:(half + 1) * 512], bank[6 + half][:], ACT.Copy)\
                .then_inc(gather_evac, 1)

        def pe_spread(pe, it, half, first=False):
            pe.wait_ge(gather_evac, it * 2 + (half + 1))
            if not first:
                pe.wait_ge(silu_ready, it * PER_GROUP)
            for jj in range(4):
                j = 4 * half + jj
                last = pe.transpose(bank[half][:, jj * P:(jj + 1) * P], hgf[:, j * P:(j + 1) * P], ident[:])
            last.then_inc(spread_ready, 1)

        def act_spread(act, it, half):
            act.wait_ge(spread_ready, it * 2 + (half + 1))
            act.activation(hg_hi[:, 4 * half:4 * half + 4, :], bank[half][:].rearrange("p (j t) -> p j t", j=4),
                           ACT.Copy).then_inc(hg_hi_ready, 1)

        def vec_spread(dve, it, half):
            dve.wait_ge(hg_hi_ready, it * 2 + (half + 1))
            dve.tensor_tensor(hg_lo[:, 4 * half:4 * half + 4, :], bank[half][:].rearrange("p (j t) -> p j t", j=4),
                              hg_hi[:, 4 * half:4 * half + 4, :].bitcast(F32), ALU.subtract)\
                .then_inc(hg_lo_ready, 1)

        def pe_slot_gate(pe, it, first=False):
            pe.wait_ge(gsel_ready, it + 1)
            if not first:
                pe.wait_ge(at_lo_ready, it * PER_GROUP)
            for t in range(NT):
                last = pe.matmul(bank[3][:, 0:PER_GROUP], place[:, t, :].bitcast(F32), gsel4[:, t, :],
                                 start=(t == 0), stop=(t == NT - 1))
            last.then_inc(slot_gate, 1)

        def vec_slot_gate(dve, it):
            dve.wait_ge(slot_gate, it + 1)
            dve.tensor_copy(gate4[:], bank[3][:, 0:PER_GROUP]).then_inc(slot_gate_evac, 1)

        def act_output(act, it):
            act.wait_ge(w_used, it * NG + NFS)
            for half in range(2):
                act.activation(ys_h[:, half * 512:(half + 1) * 512], bank[4 + half][:], ACT.Copy).then_inc(ys_hi, 1)

        def vec_output(dve, it, half):
            cols = slice(half * 512, (half + 1) * 512)
            dve.wait_ge(ys_hi, it * 2 + (half + 1))
            dve.tensor_tensor(ys_l[:, cols], bank[4 + half][:], ys_h[:, cols].bitcast(F32), ALU.subtract)\
                .then_inc(ys_lo, 1)

        def pe_combine(pe, it, t):
            if t == 0:
                pe.wait_ge(ys_lo, it * 2 + 2)
            for half in range(2):
                if t:
                    pe.wait_ge(comb_added, it * 6 + (2 * t + half - 1))
                cols = slice(half * 512, (half + 1) * 512)
                pe.matmul(bank[6 + half][:], place_t[:, t, :], ys_h[:, cols], start=True, stop=False)
                pe.matmul(bank[6 + half][:], place_t[:, t, :], ys_l[:, cols], start=False, stop=True)\
                    .then_inc(comb_ready, 1)

        def vec_combine(dve, it, t):
            for half in range(2):
                cols = slice(half * 512, (half + 1) * 512)
                dve.wait_ge(comb_ready, it * 6 + (2 * t + half + 1))
                dve.tensor_tensor(acc[:, t, cols], acc[:, t, cols], bank[6 + half][:], ALU.add)\
                    .then_inc(comb_added, 1)

        def act_group(act, it, g):
            def high(n):
                if n < NG:
                    act.wait_ge(w_landed[raw_slot(n)], it * (16 * NG // NRAW) + 16 * ((NFRONT + n) // NRAW + 1))
                    act.wait_ge(w_used, it * NG + (NFS + n - NSPLIT + 1))
                    act.activation(whi[:, split_slot(n), :], raw[:, raw_slot(n), :], ACT.Copy).then_inc(hi_ready, 1)

            for n in range(AHEAD):
                high(n)
            act_output(act, it)
            for n in range(NG):
                high(n + AHEAD)
                for e in range(PER_GROUP):
                    if n == stage_end("G", e):
                        act.wait_ge(w_used, it * NG + (NFS + n))
                        if e:
                            act.wait_ge(eact_ready, it * PER_GROUP + e)
                        act.activation(sgate, bank[e % 2][:], ACT.Silu).then_inc(silu_ready, 1)
                    if n == AT_AFTER[e] + 1:
                        act.wait_ge(at_ready, it * PER_GROUP + (e + 1))
                        act.activation(at_hi[:, e % 2], bank[3][:].rearrange("p (j s) -> p j s", j=4), ACT.Copy)\
                            .then_inc(at_hi_ready, 1)
                if n == TURN_AFTER + 1:
                    act.wait_ge(turn_ready, it + 1)
                    act.activation(place_t[:], bank[7][:, 0:TOK].rearrange("p (t s) -> p t s", t=NT), ACT.Copy)\
                        .then_inc(turn_evac, 1)
                for half in range(2):
                    if n == GATHER_AFTER[half] + 1:
                        act_gather(act, it + 1, half)
                    if n == SPREAD_AFTER[half] + 1:
                        act_spread(act, it + 1, half)

        def pe_group(pe, it, g):
            for n in range(NG):
                k, i = divmod(n, 4)
                what, e = STAGES[k]
                if what == "G" and e >= 2 and i == 0:
                    pe.wait_ge(silu_ready, it * PER_GROUP + (e - 1))
                if what == "U" and i == 0 and e:
                    pe.wait_ge(eact_ready, it * PER_GROUP + e)
                if what == "D" and i == 0:
                    pe.wait_ge(at_lo_ready, it * PER_GROUP + (e + 1))
                slot = split_slot(n)
                pe.wait_ge(lo_ready, it * NG + (NFS + n + 1))
                if what == "D":
                    for half in range(2):
                        w = slice(half * 512, (half + 1) * 512)
                        last = three(pe, bank[4 + half][:], at_hi[:, e % 2, i, :], at_lo[:, e % 2, i, :],
                                     whi[:, slot, w], wlo[:, slot, w], e == 0 and i == 0, e == 3 and i == 3)
                else:
                    if k == 0:
                        pe.wait_ge(hg_lo_ready, it * 2 + (i // 2 + 1))
                    out = bank[e % 2] if what == "G" else bank[2]
                    for jj in range(2):
                        j = 2 * i + jj
                        w = slice(jj * 512, (jj + 1) * 512)
                        last = three(pe, out[:], hg_hi[:, j, :], hg_lo[:, j, :], whi[:, slot, w],
                                     wlo[:, slot, w], j == 0, j == J - 1)
                last.then_inc(w_used, 1)
                for t in range(NT):
                    if n == COMBINE_AFTER[t]:
                        pe_combine(pe, it, t)
                if n == TURN_AFTER:
                    pe.wait_ge(comb_added, it * 6 + 6)
                    for t in range(NT):
                        last = pe.transpose(bank[7][:, t * P:(t + 1) * P], place[:, t, :].bitcast(F32), ident[:])
                    last.then_inc(turn_ready, 1)
                for half in range(2):
                    if n == GATHER_AFTER[half]:
                        pe_gather(pe, it + 1, half)
                for e in range(PER_GROUP):
                    if n == AT_AFTER[e]:
                        pe.wait_ge(eact_ready, it * PER_GROUP + (e + 1))
                        if e == 0:
                            pe.wait_ge(slot_gate_evac, it + 1)
                        for j in range(4):
                            last = pe.transpose(bank[3][:, j * P:(j + 1) * P], eact[:, j::4], ident[:])
                        last.then_inc(at_ready, 1)
                for half in range(2):
                    if n == SPREAD_AFTER[half]:
                        pe_spread(pe, it + 1, half)
                if n == SLOT_GATE_AFTER:
                    pe_slot_gate(pe, it + 1)

        def vec_group(dve, it, g):
            def low(n):
                if n < NG:
                    dve.wait_ge(hi_ready, it * NG + (NFS + n + 1))
                    dve.tensor_tensor(wlo[:, split_slot(n), :], raw[:, raw_slot(n), :],
                                      whi[:, split_slot(n), :].bitcast(F32), ALU.subtract).then_inc(lo_ready, 1)

            for n in range(AHEAD):
                low(n)
            for n in range(NG):
                if n < 2:
                    vec_output(dve, it, n)
                low(n + AHEAD)
                for t in range(NT):
                    if n == COMBINE_AFTER[t] + 1:
                        vec_combine(dve, it, t)
                if n == PLACE_AT:
                    dve.wait_ge(turn_ready, it + 1)
                    vec_place(dve, it + 1)
                    vec_gates(dve, g + 1)
                for e in range(PER_GROUP):
                    if n == stage_end("U", e):
                        dve.wait_ge(w_used, it * NG + (NFS + n))
                        dve.wait_ge(silu_ready, it * PER_GROUP + (e + 1))
                        if e:
                            dve.wait_ge(at_ready, it * PER_GROUP + e)
                        dve.scalar_tensor_tensor(out=eact, in0=bank[2][:], scalar=gate4[:, e:e + 1], in1=sgate,
                                                 op0=ALU.mult, op1=ALU.mult).then_inc(eact_ready, 1)
                    if n == AT_AFTER[e] + 1:
                        dve.wait_ge(at_hi_ready, it * PER_GROUP + (e + 1))
                        dve.tensor_tensor(at_lo[:, e % 2], bank[3][:].rearrange("p (j s) -> p j s", j=4),
                                          at_hi[:, e % 2].bitcast(F32), ALU.subtract).then_inc(at_lo_ready, 1)
                for half in range(2):
                    if n == SPREAD_AFTER[half] + 1:
                        vec_spread(dve, it + 1, half)
                if n == SLOT_GATE_AFTER + 1:
                    vec_slot_gate(dve, it + 1)
            dve.wait_ge(slot_gate_evac, it + 2)
            dve.wait_ge(comb_added, it * 6 + 6)

        def modulate(eng, j, ready):
            eng.wait_ge(xt_evac, j + 1)
            for cond, cols in ((0, slice(0, CTX)), (1, slice(CTX, TOK))):
                eng.tensor_scalar(xnt[:, j, cols], xnt[:, j, cols], scl[:, j, cond:cond + 1],
                                  shf[:, j, cond:cond + 1], ALU.mult, ALU.add).then_inc(ready, 1)

        block = ctx.enter_context(nc.Block())

        @block.sync
        def _(sp):
            sp.dma_start(craw[:, 0, :], c_ctx.rearrange("(p j) -> p j", j=J)).then_inc(cond_landed, 16)
            sp.dma_start(craw[:, 1, :], c[0].rearrange("(p j) -> p j", j=J)).then_inc(cond_landed, 16)
            load_front(sp)
            experts(sp, load_group)
            for t in range(NT):
                sp.wait_ge(y_ready, t + 1)
                sp.dma_start(y_tiles[t], y3[:, t, :]).then_inc(y_stored, 16)
            sp.wait_ge(y_stored, 16 * NT)
            sp.wait_ge(state_stored, 32)

        @block.gpsimd
        def _(pool):
            n = [0]

            def chain(ins):
                n[0] += 1
                ins.then_inc(const_step, 1)
                pool.wait_ge(const_step, n[0])

            pool.memset(wr[:], 0.0).then_inc(wr_zero, 1)
            chain(pool.memset(ident[:], 0.0))
            pool.affine_select(out=ident[:], in_=ident[:], compare_op=ALU.not_equal, fill=1.0, base=0,
                               pattern=[[-1, P]], channel_multiplier=1).then_inc(consts, 1)
            pool.memset(ones[:], 1.0).then_inc(consts, 1)
            pool.memset(eps[:], EPS).then_inc(consts, 1)
            chain(pool.memset(sel_t[:], 0.0))
            for q in range(4):
                chain(pool.affine_select(out=sel_t[:], in_=sel_t[:], compare_op=ALU.not_equal, fill=1.0,
                                         base=-32 * q, pattern=[[-1, 2]], channel_multiplier=1))
            chain(pool.memset(sel_b[:], 0.0))
            for cond in range(2):
                for row in [32 * q + cond for q in range(4)] + [2]:
                    chain(pool.affine_select(out=sel_b[:, cond, :], in_=sel_b[:, cond, :],
                                             compare_op=ALU.not_equal, fill=1.0, base=-row,
                                             pattern=[[0, P]], channel_multiplier=1))
            chain(pool.memset(sel_h[:], 0.0))
            pool.wait_ge(consts, 1)
            chain(pool.tensor_tensor(sel_e[:], ident[:, 0:EXPERTS], ident[:, 32:32 + EXPERTS], ALU.add))
            for q in (2, 3):
                chain(pool.tensor_tensor(sel_e[:], sel_e[:], ident[:, 32 * q:32 * q + EXPERTS], ALU.add))
            chain(pool.iota(int_a, [[1, P]], base=0, channel_multiplier=0))
            chain(pool.iota(int_b, [[0, P]], base=0, channel_multiplier=1))
            pool.memset(upper[:], 1.0).then_inc(consts, 1)
            pool.memset(sel_h[:].rearrange("p a b -> p (a b)")[:, 0::HEADS + 1], 1.0).then_inc(consts, 1)
            pool.wait_ge(consts, 5)
            pool.affine_select(out=upper[:], in_=upper[:], compare_op=ALU.is_ge, fill=0.0, base=-1,
                               pattern=[[1, P]], channel_multiplier=-1).then_inc(consts, 1)
            for out, pattern, base in ((iota_row[:], [[1, P]], 0), (gidx[:], [[-1, GROUPS]], GROUPS),
                                       (eidx[:], [[-1, EXPERTS]], EXPERTS), (goff[:], [[TOK, GROUPS]], 0),
                                       (base_it[:], [[P, 4], [TOK, GROUPS]], 0)):
                pool.iota(out, pattern, base=base, channel_multiplier=0,
                          allow_small_or_imprecise_dtypes=True).then_inc(consts, 1)
            assert n[0] == NCHAIN

            pool.wait_ge(mod_done, 2)
            for j in range(J // 2, J):
                modulate(pool, j, h_ready_pool)
            pool.wait_ge(lb_ready, 5)
            for w in range(8):
                d, h = divmod(w, 4)
                pool.wait_ge(proj_act, EVAC[w][0])
                f = (ff, fb)[d][:, h, :]
                k = ak[:, d, h, :]
                pool.tensor_scalar(f, f, lbt[:, 3, w:w + 1], lbt[:, 2, w:w + 1], ALU.mult, ALU.add)\
                    .then_inc(gates_ready, 1)
                pool.tensor_scalar(k, k, lbt[:, 3, w:w + 1], None, ALU.mult).then_inc(gates_ready, 1)
            pool.wait_ge(gates_ready, 16)
            for lev in range(1, LEVELS + 1):
                for d, (one, tot) in enumerate(((ff, tot_f), (fb, tot_b))):
                    src = one if lev == 1 else totals(tot, lev - 1)
                    pair = src.rearrange("p h (n two) -> p h n two", two=2)
                    if lev > 1:
                        pool.wait_ge(tots_ready, 2 * (lev - 1) + d - 1)
                    pool.tensor_tensor(totals(tot, lev), pair[:, :, :, 0], pair[:, :, :, 1], ALU.mult)\
                        .then_inc(tots_ready, 1)
            for lev in range(LEVELS):
                pool.wait_ge(kc_ready, lev + 1)
                pool.wait_ge(tots_ready, 2 * LEVELS)
                if lev:
                    pool.wait_ge(k_step, 2 * lev)
                for d in range(2):
                    keys = halves(ak[:, d], lev)[:, :, :, d, :]
                    pool.tensor_tensor(keys, keys, block_total((ff, fb)[d], (tot_f, tot_b)[d], lev, 1 - d),
                                       ALU.mult).then_inc(k_step, 1)
            pool.wait_ge(router_done, NT)
            pool.memset(acc[:], 0.0).then_inc(acc_zero, 1)

        @block.scalar
        def _(act):
            for t in range(NT):
                act.dma_start(xres[:, t, :], x_tiles[t]).then_inc(x_landed[t], 16)
            act.wait_ge(cond_landed, 32)
            act.activation(csig[:], craw[:], ACT.Sigmoid).then_inc(csig_ready, 1)
            act.dma_start(gmix[:], norm_mix_g[0].rearrange("(p j) -> p j", j=J)).then_inc(small_landed, 16)
            act.dma_start(bada[:], b_ada[0, 0:2 * D].rearrange("(v p j) -> p v j", v=2, j=J))\
                .then_inc(small_landed, 16)
            act.wait_ge(wr_zero, 1)
            act.dma_start(wr[:, :, 0:EXPERTS], w_router.rearrange("(p j) e -> p j e", j=J))\
                .then_inc(small_landed, 16)
            act.dma_start(brt[:], spread(b_router, EXPERTS)).then_inc(small_landed, 16)
            for t in range(NT):
                act.wait_ge(x_landed[t], 16)
                if t:
                    act.wait_ge(ssq_ready, t)
                act.activation(junk, xres[:, t, :], ACT.Square, accum_out=ssq[:, 0, t:t + 1]).then_inc(ssq_ready, 1)
            act.wait_ge(ssq_ready, NT)
            act.wait_ge(consts, 3)
            act.activation(std[:, 0, :], ssq[:, 0, :], ACT.Sqrt, bias=eps[:], scale=1.0 / D).then_inc(std_ready, 1)
            act.wait_ge(par_ready, 3)
            act.activation(ct[:, 0, :], bank[4][:, 0:NROW], ACT.Copy).then_inc(par_evac, 1)
            act.activation(ct[:, 1, :], bank[4][:, 64:64 + NROW], ACT.Copy).then_inc(par_evac, 1)
            act.activation(gt[:], bank[4][:, 128:140], ACT.Copy).then_inc(par_evac, 1)
            act.wait_ge(lb_ready, 1)
            act.activation(lbt[:, 0, :], lbt[:, 0, :], ACT.Exp).then_inc(lb_ready, 1)

            def ada_evacuate(blk):
                a, half = divmod(blk, 2)
                slot = ADA[a][1]
                act.wait_ge(ada_used, 4 * (blk + 1))
                act.activation(part[:, slot, half * 512:(half + 1) * 512], bank[6 + blk % 2][:], ACT.Copy)\
                    .then_inc(ada_evac, 1)
                if a >= G1 and half == 1:
                    act.wait_ge(ada_evac, blk + 1)
                    act.dma_start(part[2:3, slot, :], b_ada[0:1, ADA[a][0] * D:(ADA[a][0] + 1) * D])\
                        .then_inc(bias_landed[a - G1], 16)

            ada_evacuate(0)
            ada_evacuate(1)
            for j in range(J):
                act.wait_ge(xt_ready, j + 1)
                act.activation(xnt[:, j, :], bank[j % 4][:, 0:TOK], ACT.Copy).then_inc(xt_evac, 1)
            ada_evacuate(2)
            ada_evacuate(3)

            def high(s, slot, landed, landed_at, free_at=None):
                act.wait_ge(landed, landed_at)
                if free_at is not None:
                    act.wait_ge(w_used, free_at)
                act.activation(whi[:, s, :], raw[:, slot, :], ACT.Copy).then_inc(hi_ready, 1)

            split_chunks = [(n, x) for n, x in enumerate(FRONT) if x[0] != "ada"]

            def high_front(s):
                if s < NFS:
                    n = split_chunks[s][0]
                    high(s % NSPLIT, n % NRAW, w_landed[n % NRAW], 16 * (n // NRAW + 1),
                         s - NSPLIT + 1 if s >= NSPLIT else None)

            high_front(0)
            for j in range(J):
                if j == 5:
                    high_front(1)
                if j < J // 2:
                    act.wait_ge(h_ready, 2 * j + 2)
                else:
                    act.wait_ge(h_ready_pool, 2 * (j - J // 2) + 2)
                act.activation(lhs_hi[:, j * TOK:(j + 1) * TOK], xnt[:, j, :], ACT.Copy).then_inc(h_hi, 1)

            def assemble_keys(lev):
                if lev == 0:
                    act.wait_ge(gates_ready, 16)
                    act.wait_ge(score_ready, NT)
                    dst = ksum
                else:
                    act.wait_ge(k_step, 2 * lev)
                    act.wait_ge(q_step, 2)
                    act.wait_ge(score_ready, NT * (lev + 1))
                    dst = ff
                w = 1 << lev
                out = dst.rearrange("p h (n two w) -> p (h n) two w", two=2, w=w)
                base = ak[:, 0, 0, 0:1]
                src = bass.AP(base.tensor, base.offset, [list(base.ap[0]), [2 * w, HW // (2 * w)], [HW + w, 2],
                                                         [1, w]])
                act.activation(out, src, ACT.Copy).then_inc(kc_ready, 1)
                if lev == 1:
                    act.dma_start(s0, state_hgrn[0, 0].rearrange("d h k v -> k d h v"))\
                        .then_inc(state_landed, 16)

            def blocks_before(n):
                if n == NWIN:
                    return 12
                return sum(x[0] == "ada" for x in FRONT[:FRONT.index(("win", n))]) // 4

            blk = 4
            for n in range(NWIN):
                high_front(n + 2)
                kind, h = WIN[n]
                if kind != "i":
                    act.wait_ge(w_used, n + 1)
                    ps = bank[n % 2][:, 0:TOK]
                    if kind in ("ff", "fb"):
                        d = kind == "fb"
                        act.activation((ff, fb)[d][:, h, :], ps, ACT.Sigmoid).then_inc(proj_act, 1)
                        act.activation(ak[:, int(d), h, :], ps, ACT.Sigmoid, scale=-1.0).then_inc(proj_act, 1)
                    elif kind == "q":
                        act.activation(qh[:, h, :], ps, ACT.Sigmoid).then_inc(proj_act, 1)
                    elif kind == "bg":
                        act.activation(ub[:, h, :], ps, ACT.Sigmoid).then_inc(proj_act, 1)
                    elif kind == "g":
                        act.activation(qh[:, h, :], ps, ACT.Sigmoid).then_inc(proj_act, 1)
                    elif kind == "ac":
                        act.activation(ua[:, h, :], ps, ACT.Copy).then_inc(proj_act, 1)
                    elif kind == "ab":
                        act.activation(ab[:, h, :], ps, ACT.Copy).then_inc(proj_act, 1)
                elif h == 3:
                    act.wait_ge(w_used, n + 1)
                    for t in range(NT):
                        act.activation(v_tok[:, t, :], bank[2 + t][:], ACT.Copy).then_inc(proj_act, 1)
                done = blocks_before(n + 1)
                if 17 <= n < 17 + LEVELS:
                    assemble_keys(n - 17)
                while blk < done:
                    ada_evacuate(blk)
                    blk += 1
            high_front(NWIN + 2)
            high_front(NWIN + 3)
            for m in range(2):
                act.wait_ge(ln_centred, m + 1)
                act.activation(ub[:, m, :], yb[:, m, :], ACT.Square).then_inc(ln_sq, 1)
            act.wait_ge(kt_ready, 4)
            for k in range(4):
                act.activation(kt[:, k], bank[k][:].rearrange("p (h s) -> p h s", h=HEADS), ACT.Copy)\
                    .then_inc(kt_evac, 1)

            def y_high(k, m, src):
                act.activation(lhs_hi[:, m * TOK:(m + 1) * TOK], src, ACT.Copy).then_inc(y_hi, 1)

            for m in range(2):
                act.wait_ge(conva_step, 11 + m)
                y_high(m, m, ya[:, m, :])
            for d, out in ((0, st_out_f), (1, st_out_b)):
                act.wait_ge(kv_ready, d + 1)
                act.activation(out, bank[d][:], ACT.Copy).then_inc(kv_out, 1)
                act.wait_ge(kv_out, d + 1)
                act.dma_start(new_state[0, 0, d].rearrange("h k v -> k h v"),
                              out.rearrange("p (h v) -> p h v", h=HEADS)).then_inc(state_stored, 16)
            act.wait_ge(ln_var, 1)
            act.activation(ub[:, 0, :], bank[7][:, 0:TOK], ACT.Sqrt, bias=eps[:], scale=1.0 / 256).then_inc(ln_std, 1)
            for h in range(HEADS):
                act.wait_ge(o_ready, h + 1)
                act.activation(hn[:, h, :], bank[2 + h][:, 0:TOK], ACT.Square).then_inc(o_sq, 1)
            act.wait_ge(y_lo, 1)
            act.dma_start(row_g, spread(norm_ffn_g[0], D)).then_inc(ffn_g_landed, 16)
            act.wait_ge(o_sum, 1)
            act.activation(hr, bank[6][0:HEADS, 0:TOK], ACT.Sqrt, bias=eps[0:HEADS, :], scale=1.0 / P)\
                .then_inc(o_std, 1)
            for m in range(2):
                act.wait_ge(ln_norm, 5)
                act.activation(ub[:, m, :], yb[:, m, :], ACT.Sigmoid).then_inc(ln_sig, 1)
            for h in range(HEADS):
                act.wait_ge(o_norm, h + 1)
                y_high(2 + h, 4 + h, og[:, h, :])
            for m in range(2):
                act.wait_ge(ln_norm, 6 + m)
                y_high(6 + m, 2 + m, yb[:, m, :])

            def row_evacuate(r):
                v, cond, half = r // 4, r // 2 % 2, r % 2
                dst = {0: row_g1, 1: row_sh2, 3: row_g2}[v]
                act.wait_ge(row_ready, ROWS.index(r) + 1)
                src = bank[6 + r % 2] if r < 12 else bank[r - 12]
                act.activation(dst[:, cond, half * 512:(half + 1) * 512], src[:], ACT.Copy)\
                    .then_inc(row_act, 1)

            high_front(NWIN + 4)
            for r in range(0, 4):
                row_evacuate(r)
            for k in (5, 6, 7):
                high_front(NWIN + k)
            for r in range(4, 8):
                row_evacuate(r)
            act.wait_ge(row_dve, 4)
            act.dma_start(row_g, spread(final_norm_g, D)).then_inc(final_g_landed, 16)

            for t in range(NT):
                act.wait_ge(x2_ready, 2 * (2 * t + 2))
                act.activation(h2[:, t, :], xres[:, t, :], ACT.Square, accum_out=ssq[:, 1, t:t + 1])\
                    .then_inc(ssq_ready, 1)
                act.wait_ge(ssq_ready, NT + t + 1)
                act.activation(std[:, 1, t:t + 1], ssq[:, 1, t:t + 1], ACT.Sqrt, bias=eps[:], scale=1.0 / D)\
                    .then_inc(std_ready, 1)

            def h2_high(t):
                act.activation(lhs_hi[:, t * D:(t + 1) * D].rearrange("q (j p) -> q j p", j=J),
                               h2[:, t, :].rearrange("q (p j) -> q j p", j=J), ACT.Copy).then_inc(h2_hi, 1)

            for t in range(NT):
                act.wait_ge(h2_ready, 2 * t + 2)
                for half in range(2):
                    act.wait_ge(h2t_ready, 2 * t + half + 1)
                    act.activation(h2t[:, 4 * half:4 * half + 4, t * P:(t + 1) * P],
                                   bank[2 * t + half][:].rearrange("p (j t) -> p j t", j=4), ACT.Copy)\
                        .then_inc(h2t_evac, 1)
                if t < NT - 1:
                    h2_high(t)
            for t in range(NT):
                act.wait_ge(router_done, t + 1)
                act.activation(hgf[:, t * P:(t + 1) * P], bank[ROUTER_BANK[t]][:, 0:P], ACT.Copy)\
                    .then_inc(router_evac, 1)
            act.wait_ge(shifted, 1)
            act.activation(rt[:, 0], rt[:, 0], ACT.Exp).then_inc(exp_ready, 1)
            for r in range(12, 16):
                row_evacuate(r)
            h2_high(NT - 1)
            act.wait_ge(consts, 11)
            act.activation(place_t[:], iota_row[:].rearrange("p (o n) -> p o n", o=1).broadcast_to([P, NT, P]),
                           ACT.Copy, scale=0.0).then_inc(place_t_zero, 1)
            for half in range(2):
                act_gather(act, 0, half)
            for half in range(2):
                act_spread(act, 0, half)
            act.wait_ge(flag_ready, 1)
            done = passes(act)
            experts(act, act_group)
            act_output(act, done)
            for t in range(NT):
                act.wait_ge(x3_ready, X3_AHEAD + 2 * t + 1)
                act.activation(y3[:, t, :], xres[:, t, :], ACT.Square, accum_out=ssq[:, 2, t:t + 1])\
                    .then_inc(ssq_ready, 1)
                act.wait_ge(ssq_ready, 2 * NT + t + 1)
                act.activation(std[:, 2, t:t + 1], ssq[:, 2, t:t + 1], ACT.Sqrt, bias=eps[:], scale=1.0 / D)\
                    .then_inc(std_ready, 1)

        @block.tensor
        def _(pe):
            pe.wait_ge(csel_ready, 2)

            def ada_chunk(n, a, half, i):
                blk = 2 * a + half
                out = bank[6 + blk % 2]
                pe.wait_ge(w_landed[n % NRAW], 16 * (n // NRAW + 1))
                if i == 0 and blk >= 2:
                    pe.wait_ge(ada_evac, blk - 1)
                for jj in range(2):
                    j = 2 * i + jj
                    q = j % 4
                    last = pe.matmul(out[32 * q:32 * q + 32, :], csel[:, j, :],
                                     raw[:, n % NRAW, jj * 512:(jj + 1) * 512], start=(j < 4), stop=(j >= 4))
                last.then_inc(ada_used, 1)

            def modulation(a):
                pe.wait_ge(ada_evac, 2 * a + 2)
                if a == 0:
                    pe.wait_ge(par_evac, 3)
                for j in range(J):
                    last = pe.matmul(bank[5 - a][:, 2 * j:2 * j + 2], part[:, ADA[a][1], j::J],
                                     sel_t[:], start=True, stop=True)
                last.then_inc(mod_ready, 1)

            for n in range(8):
                ada_chunk(n, *FRONT[n][1:])
            pe.wait_ge(consts, 3)
            pe.wait_ge(const_step, NCHAIN)
            pe.wait_ge(rows_landed, 16 * 7)
            pe.transpose(bank[4][:, 0:NROW], cw[0:NROW, 0:P], ident[0:NROW, 0:NROW]).then_inc(par_ready, 1)
            pe.transpose(bank[4][:, 64:64 + NROW], cw[0:NROW, P:2 * P], ident[0:NROW, 0:NROW]).then_inc(par_ready, 1)
            pe.transpose(bank[4][:, 128:140], gw[0:12, :], ident[0:12, 0:12]).then_inc(par_ready, 1)
            for j in range(J):
                if j == 0:
                    pe.wait_ge(xn_ready, NT)
                if j >= 4:
                    pe.wait_ge(xt_evac, j - 3)
                for t in range(NT):
                    last = pe.transpose(bank[j % 4][:, t * P:(t + 1) * P], xn[:, t, j::J], ident[:])
                last.then_inc(xt_ready, 1)
            modulation(0)
            for n in range(8, 16):
                ada_chunk(n, *FRONT[n][1:])
            modulation(1)

            def scores(lev):
                if lev == 0:
                    pe.wait_ge(prep_ready, 12)
                    pe.wait_ge(proj_act, EVAC[15][0])
                else:
                    pe.wait_ge(kc_ready, lev)
                    if lev > 1:
                        pe.wait_ge(q_step, 2 * (lev - 1))
                w = 1 << max(lev - 1, 0)
                keys = ksum if lev <= 1 else ff
                for t in range(NT):
                    if lev:
                        pe.wait_ge(s_merged, NT * (lev - 1) + t + 1)
                    for h in range(HEADS):
                        out = bank[2 + t][:, h * P:(h + 1) * P]
                        at = slice(t * P, (t + 1) * P)
                        if lev == 0:
                            rhs = qh[:, h, at]
                        else:
                            base = aq[:, 0, h, t * P:t * P + 1]
                            rhs = bass.AP(base.tensor, base.offset,
                                          [list(base.ap[0]), [2 * w, P // (2 * w)], [HW + w, 2], [1, w]])
                            out = out.rearrange("p (n two w) -> p n two w", two=2, w=w)
                        last = pe.matmul(out, keys[:, h, at], rhs, start=True, stop=True)
                    last.then_inc(score_ready, 1)

            def wait_split(s):
                pe.wait_ge(lo_ready, s + 1)

            def win_chunk(n):
                kind, h = WIN[n]
                s = n
                slot = s % NSPLIT
                wait_split(s)
                if kind != "i":
                    m = n - 2
                    while m >= 0 and WIN[m][0] == "i":
                        m -= 2
                    if m >= 0:
                        if act_ops(WIN[m][0])[1]:
                            pe.wait_ge(proj_dve, EVAC[m][1])
                        else:
                            pe.wait_ge(proj_act, EVAC[m][0])
                    for j in range(J):
                        if n == 0:
                            pe.wait_ge(h_lo, j + 1)
                        w = slice(j * P, (j + 1) * P)
                        x = slice(j * TOK, (j + 1) * TOK)
                        last = three(pe, bank[n % 2][:, 0:TOK], whi[:, slot, w], wlo[:, slot, w],
                                     lhs_hi[:, x], lhs_lo[:, x], j == 0, j == J - 1)
                else:
                    for jj in range(2):
                        j = 2 * h + jj
                        w = slice(jj * 512, (jj + 1) * 512)
                        for t in range(NT):
                            x = slice(j * TOK + t * P, j * TOK + (t + 1) * P)
                            last = three(pe, bank[2 + t][:], lhs_hi[:, x], lhs_lo[:, x],
                                         whi[:, slot, w], wlo[:, slot, w], j == 0, j == J - 1)
                last.then_inc(w_used, 1)

            for n in range(16, NFRONT - 8):
                x = FRONT[n]
                if x[0] == "ada":
                    ada_chunk(n, *x[1:])
                else:
                    win_chunk(x[1])
                    if x[1] >= 17 and x[1] <= 17 + LEVELS:
                        scores(x[1] - 17)
            pe.wait_ge(convb_step, 2 * NTAPB)
            pe.wait_ge(ada_evac, 12)
            for m in range(2):
                last = pe.matmul(bank[6][:, 0:TOK], ones[:], yb[:, m, :], start=(m == 0), stop=(m == 1))
            last.then_inc(ln_mean, 1)
            pe.wait_ge(k_step, 2 * LEVELS)
            pe.wait_ge(s_merged, NT * (LEVELS + 1))
            pe.wait_ge(proj_act, EVAC[NWIN - 1][0])
            groups = [(0, 0), (1, 0), (0, 1), (1, 2)]
            for k, (d, t) in enumerate(groups):
                for h in range(HEADS):
                    last = pe.transpose(bank[k][:, h * P:(h + 1) * P], ak[:, d, h, t * P:(t + 1) * P], ident[:])
                last.then_inc(kt_ready, 1)
            pe.wait_ge(ln_sq, 2)
            for m in range(2):
                last = pe.matmul(bank[7][:, 0:TOK], ones[:], ub[:, m, :], start=(m == 0), stop=(m == 1))
            last.then_inc(ln_var, 1)
            for k, (d, t) in enumerate(groups):
                pe.wait_ge(kt_evac, k + 1)
                for h in range(HEADS):
                    last = pe.matmul(bank[k][:, h * P:(h + 1) * P], kt[:, k, h, :],
                                     v_tok[:, t, h * P:(h + 1) * P], start=True, stop=True)
                last.then_inc(kv_ready, 1)
            def from_scores(h):
                for t in range(NT):
                    pe.matmul(bank[2 + h][:, t * P:(t + 1) * P], v_tok[:, t, h * P:(h + 1) * P], smat[:, t, h, :],
                              start=(t == 0), stop=False)

            pe.wait_ge(proj_act, EVAC[NWIN - 1][0])
            for h in (2, 3):
                from_scores(h)
            pe.wait_ge(state_landed, 16)
            pe.wait_ge(q_step, 2 * LEVELS)
            pe.wait_ge(state_ready, 8)

            def head_sum(h):
                pe.wait_ge(o_sq, h + 1)
                if h == 0:
                    pe.wait_ge(ln_centred, 2)
                last = pe.matmul(bank[6][0:HEADS, 0:TOK], sel_h[:, h, :], hn[:, h, :], start=(h == 0),
                                 stop=(h == HEADS - 1))
                if h == HEADS - 1:
                    last.then_inc(o_sum, 1)

            for h in range(HEADS):
                out = bank[2 + h]
                hs = slice(h * P, (h + 1) * P)
                if h < 2:
                    from_scores(h)
                for t in (1, 2):
                    at = slice(t * P, (t + 1) * P)
                    before = s0[:, 0, hs] if t == 1 else sf2[:, h, :]
                    after = sb1[:, h, :] if t == 1 else s0[:, 1, hs]
                    pe.matmul(out[:, at], before, aq[:, 1, h, at], start=False, stop=False)
                    last = pe.matmul(out[:, at], after, aq[:, 0, h, at], start=False, stop=(t == 2))
                last.then_inc(o_ready, 1)
                if h:
                    head_sum(h - 1)
            head_sum(HEADS - 1)

            def row(r):
                v = r // 4
                if r % 4 == 0:
                    pe.wait_ge(bias_landed[v], 16)
                if r < 2:
                    pe.wait_ge(o_norm, HEADS - 1 + r)
                else:
                    was = ROWS.index(r) - 2
                    kinds = [ROWS[x] // 4 == 2 for x in range(was + 1)]
                    if kinds[-1]:
                        pe.wait_ge(row_dve, sum(kinds))
                    else:
                        pe.wait_ge(row_act, was + 1 - sum(kinds))
                spread_row(bank[6 + r % 2], r)

            def spread_row(out, r):
                v, cond, half = r // 4, r // 2 % 2, r % 2
                pe.matmul(out[:], sel_b[:, cond, :], part[:, ADA[G1 + v][1], half * 512:(half + 1) * 512],
                          start=True, stop=True).then_inc(row_ready, 1)

            def head_spread(h):
                pe.wait_ge(o_rstd, 1)
                if h == 0:
                    pe.wait_ge(o_std, 1)
                if h == 1:
                    pe.wait_ge(ln_std, 1)
                if h >= 2:
                    pe.wait_ge(o_norm, h - 1)
                pe.matmul(bank[6 + h % 2][:, 0:TOK], ident[0:HEADS, h:h + 1].broadcast_to([HEADS, P]), hr,
                          start=True, stop=True).then_inc(o_spread, 1)

            def out_chunk(k, t):
                s, m = NWIN + k, WOUT[k]
                for half in range(2):
                    x = slice(m * TOK + t * P, m * TOK + (t + 1) * P)
                    w = slice(half * 512, (half + 1) * 512)
                    last = three(pe, bank[2 * t + half][:], lhs_hi[:, x], lhs_lo[:, x],
                                 whi[:, s % NSPLIT, w], wlo[:, s % NSPLIT, w], k == 0, k == 7)
                return last

            pe.wait_ge(kv_out, 2)
            pe.wait_ge(o_gated, HEADS)
            for k in range(8 - OUT_TAIL):
                wait_split(NWIN + k)
                pe.wait_ge(y_lo, k + 1)
                for t in range(NT):
                    last = out_chunk(k, t)
                last.then_inc(w_used, 1)
                if k == 0:
                    for h in range(HEADS):
                        head_spread(h)
                else:
                    for r in ROWS[4 * k - 4:4 * k]:
                        row(r)
            for t in range(NT):
                for k in range(8 - OUT_TAIL, 8):
                    if t == 0:
                        wait_split(NWIN + k)
                        pe.wait_ge(y_lo, k + 1)
                    last = out_chunk(k, t)
                    if t == NT - 1:
                        last.then_inc(w_used, 1)
                if t < NT - 1:
                    last.then_inc(tile_done, 1)
            def turn_h2(t):
                pe.wait_ge(h2_ready, 2 * t + 2)
                for half in range(2):
                    for jj in range(4):
                        j = 4 * half + jj
                        last = pe.transpose(bank[2 * t + half][:, jj * P:(jj + 1) * P], h2[:, t, j::J], ident[:])
                    last.then_inc(h2t_ready, 1)

            def router(t):
                if t == 0:
                    pe.wait_ge(small_landed, 64)
                    pe.wait_ge(row_act, 8)
                pe.wait_ge(h2t_evac, 2 * t + 2)
                at = slice(t * P, (t + 1) * P)
                for j in range(J):
                    q = j % 4
                    last = pe.matmul(bank[ROUTER_BANK[t]][32 * q:32 * q + 32, 0:P], wr[:, j, :], h2t[:, j, at],
                                     start=(j < 4), stop=(j >= 4))
                last.then_inc(router_done, 1)

            turn_h2(0)
            turn_h2(1)
            router(0)
            turn_h2(2)
            router(1)
            router(2)
            for t in range(NT):
                pe.wait_ge(router_evac, t + 1)
                last = pe.matmul(bank[7][:, t * EXPERTS:(t + 1) * EXPERTS], hgf[:, t * P:(t + 1) * P], sel_e[:],
                                 start=True, stop=True)
            last.then_inc(logits_ready, 1)
            pe.wait_ge(bias_landed[3], 16)
            for r in ROWS[12:]:
                spread_row(bank[r - 12], r)
            pe.wait_ge(group_ready, 1)
            pe.wait_ge(consts, 11)
            gsel = rt[:, 3, :, 0:GROUPS]
            rank = bank[7][:, 0:NT * GROUPS]
            pe.matmul(rank.rearrange("p (t g) -> p t g", g=GROUPS), upper[:], gsel, start=True, stop=False)
            for a, b in ((0, 1), (0, 2), (1, 2)):
                pe.matmul(rank[:, b * GROUPS:(b + 1) * GROUPS], ones[:], gsel[:, a, :], start=False,
                          stop=(b == 2 and a == 1))
            for t in range(NT):
                last = pe.matmul(bank[5][:, 0:GROUPS], ones[:], gsel[:, t, :], start=(t == 0), stop=(t == NT - 1))
            last.then_inc(rank_ready, 1)
            pe.wait_ge(h2_lo, NT)
            for half in range(2):
                pe_gather(pe, 0, half, first=True)
            pe.wait_ge(row_act, 12)
            for half in range(2):
                pe_spread(pe, 0, half, first=True)
            pe_slot_gate(pe, 0, first=True)
            pe.wait_ge(place_t_zero, 1)
            done = passes(pe)
            experts(pe, pe_group)
            for t in range(NT):
                pe_combine(pe, done, t)

        @block.vector
        def _(dve):
            n_step = [0]

            def step(ins):
                n_step[0] += 1
                ins.then_inc(vec_step, 1)
                dve.wait_ge(vec_step, n_step[0])

            step(dve.memset(csel[:], 0.0))
            dve.wait_ge(csig_ready, 1)
            for cond in range(2):
                dve.tensor_tensor(csel[:, :, cond:cond + 1].rearrange("p j o -> p (j o)"), craw[:, cond, :],
                                  csig[:, cond, :], ALU.mult).then_inc(csel_ready, 1)
            dve.wait_ge(const_step, NCHAIN)
            step(dve.tensor_tensor(int_c, int_a, int_b, ALU.bitwise_xor))
            for lev in range(LEVELS):
                dve.tensor_single_scalar(masks[:, lev, :], int_c, 1 << lev, ALU.is_ge).then_inc(masks_ready, 1)
            dve.wait_ge(std_ready, 1)
            dve.reciprocal(rstd[:, 0, :], std[:, 0, :]).then_inc(rstd_ready, 1)
            dve.wait_ge(rstd_ready, 1)
            for t in range(NT):
                dve.tensor_scalar(xn[:, t, :], xres[:, t, :], rstd[:, 0, t:t + 1], None, ALU.mult)\
                    .then_inc(xn_ready, 1)
            dve.wait_ge(par_evac, 3)
            dve.tensor_tensor(lbt[:, 0, :], gt[:, 4:12], gt[:, 4:12], ALU.subtract).then_inc(lb_ready, 1)
            dve.wait_ge(lb_ready, 2)
            step(dve.reciprocal(lbt[:, 1, :], lbt[:, 0, :]))
            dve.tensor_tensor(lbt[:, 1, :], lbt[:, 0, :], lbt[:, 1, :], ALU.mult).then_inc(lb_ready, 1)
            dve.wait_ge(lb_ready, 3)
            dve.tensor_tensor(lbt[:, 2, :], lbt[:, 1, :], lbt[:, 1, :], ALU.subtract).then_inc(lb_ready, 1)
            dve.wait_ge(lb_ready, 4)
            dve.tensor_scalar(lbt[:, 3, :], lbt[:, 2, :], -1.0, 1.0, ALU.mult, ALU.add).then_inc(lb_ready, 1)

            def per_cond(v):
                return v.rearrange("p (j o) -> p j o", o=1).broadcast_to([P, J, 2])

            dve.wait_ge(small_landed, 64)
            dve.wait_ge(mod_ready, 1)
            step(dve.tensor_tensor(scl[:], bank[5][:, 0:16].rearrange("p (j c) -> p j c", c=2),
                                   per_cond(bada[:, 1, :]), ALU.add))
            dve.scalar_tensor_tensor(out=scl[:], in0=scl[:], scalar=1.0, in1=per_cond(gmix[:]), op0=ALU.add,
                                     op1=ALU.mult).then_inc(mod_done, 1)
            def low(s, slot, at):
                dve.wait_ge(hi_ready, at)
                dve.tensor_tensor(wlo[:, s, :], raw[:, slot, :], whi[:, s, :].bitcast(F32), ALU.subtract)\
                    .then_inc(lo_ready, 1)

            split_raw = [n for n, x in enumerate(FRONT) if x[0] != "ada"]

            def low_front(s):
                if s < NFS:
                    low(s % NSPLIT, split_raw[s] % NRAW, s + 1)

            low_front(0)
            dve.wait_ge(mod_ready, 2)
            dve.tensor_tensor(shf[:], bank[4][:, 0:16].rearrange("p (j c) -> p j c", c=2),
                              per_cond(bada[:, 0, :]), ALU.add).then_inc(mod_done, 1)
            dve.wait_ge(mod_done, 2)

            def h_low(j):
                dve.wait_ge(h_hi, j + 1)
                x = slice(j * TOK, (j + 1) * TOK)
                dve.tensor_tensor(lhs_lo[:, x], xnt[:, j, :], lhs_hi[:, x].bitcast(F32), ALU.subtract)\
                    .then_inc(h_lo, 1)

            for j in range(J // 2):
                modulate(dve, j, h_ready)
                if j:
                    h_low(j - 1)
            for j in range(J // 2 - 1, J):
                if j == 6:
                    low_front(1)
                h_low(j)

            def merge(lev):
                for t in range(NT):
                    dve.wait_ge(score_ready, NT * lev + t + 1)
                    src = bank[2 + t][:].rearrange("p (h t) -> p h t", h=HEADS)
                    if lev == 0:
                        dve.tensor_copy(smat[:, t], src).then_inc(s_merged, 1)
                    else:
                        dve.wait_ge(s_merged, NT * (lev - 1) + t + 1)
                        mask = masks[:, lev - 1:lev, :].broadcast_to([P, HEADS, P])
                        dve.copy_predicated(smat[:, t], mask, src).then_inc(s_merged, 1)

            def decay_queries(lev):
                dve.wait_ge(tots_ready, 2 * LEVELS)
                if lev:
                    dve.wait_ge(q_step, 2 * lev)
                for d in range(2):
                    x = halves(aq[:, 1 - d], lev)[:, :, :, 1 - d, :]
                    dve.tensor_tensor(x, x, block_total((ff, fb)[d], (tot_f, tot_b)[d], lev, d), ALU.mult)\
                        .then_inc(q_step, 1)

            w_a = lambda m, k: ct[:, m, k:k + 1]
            w_b = lambda m, k: ct[:, m, CONV_A + k:CONV_A + k + 1]
            extra = lambda m, k: ct[:, m, CONV_A + CONV_B + k:CONV_A + CONV_B + k + 1]
            nb = [0]

            def conv_b(first, last):
                for tap in range(first, last):
                    for m in range(2):
                        u, y = ub[:, m, :], yb[:, m, :]
                        nb[0] += 1
                        if nb[0] > 2:
                            dve.wait_ge(convb_step, nb[0] - 2)
                        if tap == 0:
                            dve.tensor_scalar(y, u, w_b(m, CONV_B // 2), extra(m, 0), ALU.mult, ALU.add)\
                                .then_inc(convb_step, 1)
                            continue
                        along, d = TAPS_B[tap]
                        if along == "time":
                            lo, hi, shift = max(0, -d), min(CTX, CTX - d), d
                        else:
                            lo, hi = CTX + max(0, -d) * GRID_W, TOK - max(0, d) * GRID_W
                            shift = d * GRID_W
                        w = w_b(m, CONV_B // 2 + d)
                        dve.scalar_tensor_tensor(out=y[:, lo:hi], in0=u[:, lo + shift:hi + shift], scalar=w,
                                                 in1=y[:, lo:hi], op0=ALU.mult, op1=ALU.add)\
                            .then_inc(convb_step, 1)

            def conv_a():
                for m in range(2):
                    dve.tensor_scalar(ya[:, m, :], ua[:, m, :], w_a(m, 1), None, ALU.mult).then_inc(conva_step, 1)
                for d in (-1, 1):
                    for m in range(2):
                        y, u = ya[:, m, :], ua[:, m, :]
                        dve.wait_ge(conva_step, 2 if d < 0 else 6)
                        rows_y = y[:, CTX:TOK].rearrange("p (r w) -> p r w", w=GRID_W)
                        rows_u = u[:, CTX:TOK].rearrange("p (r w) -> p r w", w=GRID_W)
                        lo, hi = max(0, -d), GRID_W - max(0, d)
                        dve.scalar_tensor_tensor(out=rows_y[:, :, lo:hi], in0=rows_u[:, :, lo + d:hi + d],
                                                 scalar=w_a(m, 1 + d), in1=rows_y[:, :, lo:hi], op0=ALU.mult,
                                                 op1=ALU.add).then_inc(conva_step, 1)
                        lo, hi = max(0, -d), CTX - max(0, d)
                        dve.scalar_tensor_tensor(out=y[:, lo:hi], in0=u[:, lo + d:hi + d], scalar=w_a(m, 1 + d),
                                                 in1=y[:, lo:hi], op0=ALU.mult, op1=ALU.add)\
                            .then_inc(conva_step, 1)

            for n in range(NWIN):
                low_front(n + 2)
                kind, h = WIN[n]
                ps = bank[n % 2][:, 0:TOK]
                if kind in ("q", "ba", "g", "ax"):
                    dve.wait_ge(w_used, n + 1)
                    if kind in ("q", "g"):
                        dve.wait_ge(proj_act, EVAC[n][0])
                if kind == "q":
                    dve.scalar_tensor_tensor(out=qh[:, h, :], in0=ps, scalar=float(P) ** -0.5, in1=qh[:, h, :],
                                             op0=ALU.mult, op1=ALU.mult).then_inc(proj_dve, 1)
                    dve.wait_ge(proj_dve, EVAC[n][1])
                    dve.wait_ge(gates_ready, 8 + 2 * h + 2)
                    dve.tensor_tensor(ksum[:, h, :], ak[:, 0, h, :], ak[:, 1, h, :], ALU.add).then_inc(prep_ready, 1)
                    dve.tensor_tensor(aq[:, 1, h, :], qh[:, h, :], ff[:, h, :], ALU.mult).then_inc(prep_ready, 1)
                    dve.tensor_tensor(aq[:, 0, h, :], qh[:, h, :], fb[:, h, :], ALU.mult).then_inc(prep_ready, 1)
                elif kind == "ba":
                    dve.wait_ge(proj_act, EVAC[17][0])
                    dve.tensor_tensor(ub[:, h, :], ps, ub[:, h, :], ALU.mult).then_inc(proj_dve, 1)
                elif kind == "g":
                    dve.scalar_tensor_tensor(out=qh[:, h, :], in0=ps, scalar=gt[:, h:h + 1], in1=qh[:, h, :],
                                             op0=ALU.mult, op1=ALU.mult).then_inc(proj_dve, 1)
                elif kind == "ax":
                    dve.wait_ge(proj_act, EVAC[25][0])
                    dve.tensor_tensor(ua[:, h, :], ps, ua[:, h, :], ALU.mult).then_inc(proj_dve, 1)
                if n == 17:
                    dve.wait_ge(masks_ready, LEVELS)
                    dve.wait_ge(prep_ready, 12)
                if 17 <= n <= 17 + LEVELS:
                    merge(n - 17)
                    if n > 17:
                        decay_queries(n - 18)
                if n == 19:
                    dve.wait_ge(proj_dve, EVAC[19][1])
                if n >= 19:
                    per = -(-NTAPB // (NWIN - 19))
                    conv_b(min(NTAPB, (n - 19) * per), min(NTAPB, (n - 18) * per))
                if n == 27:
                    dve.wait_ge(proj_dve, EVAC[27][1])
                    dve.wait_ge(convb_step, nb[0])
                    conv_a()
            for m in range(2):
                dve.wait_ge(ln_mean, 1)
                dve.scalar_tensor_tensor(out=yb[:, m, :], in0=bank[6][:, 0:TOK], scalar=-1.0 / 256,
                                         in1=yb[:, m, :], op0=ALU.mult, op1=ALU.add).then_inc(ln_centred, 1)
            dve.wait_ge(proj_act, EVAC[NWIN - 1][0])
            dve.wait_ge(conva_step, 10)
            for m in range(2):
                dve.tensor_tensor(ya[:, m, :], ya[:, m, :], ab[:, m, :], ALU.mult).then_inc(conva_step, 1)

            def y_low(k, m, src):
                dve.wait_ge(y_hi, k + 1)
                x = slice(m * TOK, (m + 1) * TOK)
                dve.tensor_tensor(lhs_lo[:, x], src, lhs_hi[:, x].bitcast(F32), ALU.subtract).then_inc(y_lo, 1)

            low_front(NWIN + 2)
            low_front(NWIN + 3)
            dve.wait_ge(state_landed, 16)
            for d, (tot, t, old, new) in enumerate(((tot_f, 1, s0[:, 0, :], sf2), (tot_b, 2, s0[:, 1, :], sb1))):
                dve.wait_ge(kv_ready, 3 + d)
                for h in range(HEADS):
                    dve.scalar_tensor_tensor(out=new[:, h, :], in0=old[:, h * P:(h + 1) * P],
                                             scalar=totals(tot, LEVELS)[:, h, t:t + 1],
                                             in1=bank[2 + d][:, h * P:(h + 1) * P], op0=ALU.mult, op1=ALU.add)\
                        .then_inc(state_ready, 1)
            for m in range(2):
                y_low(m, m, ya[:, m, :])
            dve.wait_ge(ln_std, 1)
            dve.reciprocal(ub[:, 0, :], ub[:, 0, :]).then_inc(ln_norm, 1)

            def head_gate(h):
                dve.wait_ge(o_sq, h + 1)
                dve.tensor_tensor(og[:, h, :], bank[2 + h][:, 0:TOK], qh[:, h, :], ALU.mult).then_inc(o_gated, 1)

            for h in range(HEADS):
                head_gate(h)
            dve.wait_ge(o_std, 1)
            dve.reciprocal(hr, hr).then_inc(o_rstd, 1)
            for m in range(2):
                dve.wait_ge(ln_norm, 1 + 2 * m)
                dve.tensor_tensor(yb[:, m, :], yb[:, m, :], ub[:, 0, :], ALU.mult).then_inc(ln_norm, 1)
                dve.wait_ge(ln_norm, 2 + 2 * m)
                dve.tensor_scalar(yb[:, m, :], yb[:, m, :], extra(m, 1), extra(m, 2), ALU.mult, ALU.add)\
                    .then_inc(ln_norm, 1)
            for h in range(HEADS + 1):
                if h < HEADS:
                    dve.wait_ge(o_spread, h + 1)
                    dve.wait_ge(o_gated, h + 1)
                    dve.tensor_tensor(og[:, h, :], og[:, h, :], bank[6 + h % 2][:, 0:TOK], ALU.mult)\
                        .then_inc(o_norm, 1)
                if h:
                    dve.wait_ge(o_norm, h)
                    y_low(1 + h, 3 + h, og[:, h - 1, :])
            for m in range(2):
                dve.wait_ge(ln_sig, 2)
                dve.tensor_tensor(yb[:, m, :], yb[:, m, :], ub[:, m, :], ALU.mult).then_inc(ln_norm, 1)
            for m in range(2):
                dve.wait_ge(ln_norm, 6 + m)
                y_low(6 + m, 2 + m, yb[:, m, :])
            low_front(NWIN + 4)
            low_front(NWIN + 5)
            dve.wait_ge(ffn_g_landed, 16)
            for r in range(8, 12):
                cond, half = r // 2 % 2, r % 2
                cols = slice(half * 512, (half + 1) * 512)
                dve.wait_ge(row_ready, ROWS.index(r) + 1)
                dve.scalar_tensor_tensor(out=row_sc2[:, cond, cols], in0=bank[6 + r % 2][:], scalar=1.0,
                                         in1=row_g[:, cols], op0=ALU.add, op1=ALU.mult).then_inc(row_dve, 1)
            low_front(NWIN + 6)
            low_front(NWIN + 7)

            def residual(t):
                if t < NT - 1:
                    dve.wait_ge(tile_done, t + 1)
                else:
                    dve.wait_ge(w_used, NFS)
                dve.wait_ge(row_act, 4)
                for half in range(2):
                    cols = slice(half * 512, (half + 1) * 512)
                    dve.tensor_tensor(h2[:, t, cols], bank[2 * t + half][:], row_g1[:, COND[t], cols], ALU.mult)\
                        .then_inc(x2_ready, 1)
                for half in range(2):
                    cols = slice(half * 512, (half + 1) * 512)
                    dve.wait_ge(x2_ready, 4 * t + half + 1)
                    dve.tensor_tensor(xres[:, t, cols], xres[:, t, cols], h2[:, t, cols], ALU.add)\
                        .then_inc(x2_ready, 1)

            def ffn_input(t):
                dve.wait_ge(row_dve, 4)
                dve.wait_ge(row_act, 8)
                dve.wait_ge(std_ready, 2 + t)
                dve.reciprocal(rstd[:, 1, t:t + 1], std[:, 1, t:t + 1]).then_inc(rstd_ready, 1)
                dve.wait_ge(rstd_ready, 2 + t)
                dve.scalar_tensor_tensor(out=h2[:, t, :], in0=xres[:, t, :], scalar=rstd[:, 1, t:t + 1],
                                         in1=row_sc2[:, COND[t], :], op0=ALU.mult, op1=ALU.mult)\
                    .then_inc(h2_ready, 1)
                dve.wait_ge(h2_ready, 2 * t + 1)
                dve.tensor_tensor(h2[:, t, :], h2[:, t, :], row_sh2[:, COND[t], :], ALU.add).then_inc(h2_ready, 1)

            residual(0)
            ffn_input(0)
            residual(1)
            residual(2)
            ffn_input(1)
            ffn_input(2)
            def h2_low(t):
                dve.wait_ge(h2_hi, t + 1)
                x = slice(t * D, (t + 1) * D)
                dve.tensor_tensor(lhs_lo[:, x].rearrange("q (j p) -> q j p", j=J),
                                  h2[:, t, :].rearrange("q (p j) -> q j p", j=J),
                                  lhs_hi[:, x].bitcast(F32).rearrange("q (j p) -> q j p", j=J), ALU.subtract)\
                    .then_inc(h2_lo, 1)

            for t in range(NT - 1):
                h2_low(t)

            def r3(k, n=EXPERTS):
                return rt[:, k, :, 0:n]

            def one(k):
                return rt[:, k, :, 0:1]

            def bc(k, n):
                return one(k).broadcast_to([P, NT, n])

            def table(t, n):
                return t[:].rearrange("p (o n) -> p o n", o=1).broadcast_to([P, NT, n])

            logits = bank[7][:, 0:NT * EXPERTS].rearrange("p (t e) -> p t e", e=EXPERTS)
            dve.wait_ge(logits_ready, 1)
            step(dve.tensor_reduce(one(1), logits, AX, ALU.max))
            dve.tensor_tensor(r3(0), logits, bc(1, EXPERTS), ALU.subtract).then_inc(shifted, 1)
            dve.wait_ge(exp_ready, 1)
            step(dve.tensor_reduce(one(1), r3(0), AX, ALU.add))
            step(dve.reciprocal(one(1), one(1)))
            step(dve.tensor_tensor(r3(0), r3(0), bc(1, EXPERTS), ALU.mult))
            step(dve.tensor_tensor(r3(2), r3(0), table(brt, EXPERTS), ALU.add))
            v = rt[:, 2].rearrange("p t (g e) -> p (t g) e", g=GROUPS)
            at = 0
            for far in (1, 2, 3):
                m = PER_GROUP - far
                ins = dve.tensor_tensor(rpair[:, :, at:at + m], v[:, :, 0:m], v[:, :, far:PER_GROUP], ALU.add)
                at += m
                n_step[0] += 1
                ins.then_inc(vec_step, 1)
            dve.wait_ge(vec_step, n_step[0])
            gs = rt[:, 4].rearrange("p t e -> p (t e)")[:, 0:NT * GROUPS]
            gs3 = gs.rearrange("p (t g) -> p t g", g=GROUPS)
            step(dve.tensor_reduce(gs.rearrange("p (a o) -> p a o", o=1), rpair[:], AX, ALU.max))

            def first_max(out, values, scratch, m, order, n):
                step(dve.tensor_reduce(one(m), values, AX, ALU.max))
                step(dve.tensor_tensor(scratch, values, bc(m, n), ALU.is_equal))
                step(dve.tensor_tensor(scratch, scratch, table(order, n), ALU.mult))
                step(dve.tensor_reduce(one(m), scratch, AX, ALU.max))
                return dve.tensor_tensor(out, scratch, bc(m, n), ALU.is_equal)

            first_max(r3(3, GROUPS), gs3, r3(5, GROUPS), 1, gidx, GROUPS).then_inc(group_ready, 1)
            dve.wait_ge(group_ready, 1)
            ing = rt[:, 3, :, 0:GROUPS].rearrange("p t (g o) -> p t g o", o=1)\
                .broadcast_to([P, NT, GROUPS, PER_GROUP])
            four = lambda k: rt[:, k].rearrange("p t (g e) -> p t g e", g=GROUPS)
            step(dve.tensor_tensor(four(6), four(2), ing, ALU.mult))
            step(dve.tensor_scalar(r3(7, GROUPS), r3(3, GROUPS), 1e9, -1e9, ALU.mult, ALU.add))
            out_of = rt[:, 7, :, 0:GROUPS].rearrange("p t (g o) -> p t g o", o=1)\
                .broadcast_to([P, NT, GROUPS, PER_GROUP])
            step(dve.tensor_tensor(four(6), four(6), out_of, ALU.add))
            step(first_max(r3(8), r3(6), r3(5), 1, eidx, EXPERTS))
            dve.wait_ge(rank_ready, 1)
            rank = bank[7][:, 0:NT * GROUPS].rearrange("p (t g) -> p t g", g=GROUPS)
            step(dve.tensor_tensor(r3(10, GROUPS), rank, table(goff, GROUPS), ALU.add))
            step(dve.tensor_tensor(r3(10, GROUPS), r3(10, GROUPS), r3(3, GROUPS), ALU.mult))
            step(dve.tensor_reduce(code[:].rearrange("p (t o) -> p t o", o=1), r3(10, GROUPS), AX, ALU.add))
            step(dve.tensor_tensor(codem[:], code[:].rearrange("p (t o) -> p t o", o=1)
                                   .broadcast_to([P, NT, 4 * GROUPS]),
                                   base_it[:].rearrange("p (o n) -> p o n", o=1).broadcast_to([P, NT, 4 * GROUPS]),
                                   ALU.subtract))
            vec_place(dve, 0)
            h2_low(NT - 1)
            step(dve.scalar_tensor_tensor(out=r3(6), in0=r3(8), scalar=-3e9, in1=r3(6), op0=ALU.mult, op1=ALU.add))
            step(first_max(r3(9), r3(6), r3(5), 1, eidx, EXPERTS))
            step(dve.tensor_tensor(r3(8), r3(8), r3(9), ALU.add))
            step(dve.tensor_tensor(r3(8), r3(8), r3(0), ALU.mult))
            step(dve.tensor_reduce(one(1), r3(8), AX, ALU.add))
            step(dve.reciprocal(one(1), one(1)))
            step(dve.tensor_tensor(gates[:, :, 0:EXPERTS], r3(8), bc(1, EXPERTS), ALU.mult))
            step(dve.tensor_copy(gates[:, :, EXPERTS:], gates[:, :, 0:PER_GROUP]))
            vec_gates(dve, 0)
            step(dve.tensor_reduce(flagf[:], bank[5][:, 0:GROUPS], AX, ALU.max))
            dve.tensor_scalar(flag[:], flagf[:], float(P), None, ALU.is_gt).then_inc(flag_ready, 1)
            for half in range(2):
                vec_spread(dve, 0, half)
            vec_slot_gate(dve, 0)
            dve.wait_ge(acc_zero, 1)
            done = passes(dve)
            experts(dve, vec_group)
            dve.wait_ge(row_act, 12)
            dve.wait_ge(final_g_landed, 16)

            def x3(out, a, b, op):
                n_x3[0] += 1
                dve.tensor_tensor(out, a, b, op).then_inc(x3_ready, 1)
                dve.wait_ge(x3_ready, n_x3[0])

            n_x3 = [0]
            x3(acc[:, 0, :], acc[:, 0, :], row_g2[:, COND[0], :], ALU.mult)
            x3(xres[:, 0, :], xres[:, 0, :], acc[:, 0, :], ALU.add)
            assert n_x3[0] == X3_AHEAD
            for half in range(2):
                vec_output(dve, done, half)

            def last_output(t):
                if t == 0:
                    for half in range(2):
                        cols = slice(half * 512, (half + 1) * 512)
                        dve.wait_ge(comb_ready, done * 6 + (half + 1))
                        dve.tensor_tensor(acc[:, 0, cols], bank[6 + half][:], row_g2[:, COND[0], cols], ALU.mult)\
                            .then_inc(comb_added, 1)
                    dve.wait_ge(comb_added, done * 6 + 2)
                else:
                    vec_combine(dve, done, t)
                    dve.wait_ge(comb_added, done * 6 + (2 * t + 2))
                    x3(acc[:, t, :], acc[:, t, :], row_g2[:, COND[t], :], ALU.mult)
                n_x3[0] += 1
                dve.tensor_tensor(xres[:, t, :], xres[:, t, :], acc[:, t, :], ALU.add).then_inc(x3_ready, 1)

            def final_norm(t):
                dve.wait_ge(std_ready, 1 + NT + t + 1)
                dve.reciprocal(rstd[:, 2, t:t + 1], std[:, 2, t:t + 1]).then_inc(rstd_ready, 1)
                dve.wait_ge(rstd_ready, 1 + NT + t + 1)
                dve.scalar_tensor_tensor(out=y3[:, t, :], in0=xres[:, t, :], scalar=rstd[:, 2, t:t + 1],
                                         in1=row_g, op0=ALU.mult, op1=ALU.mult).then_inc(y_ready, 1)

            last_output(0)
            last_output(1)
            final_norm(0)
            last_output(2)
            final_norm(1)
            final_norm(2)

_INS = ["x_prompt", "x_sample", "state_hgrn", "c", "c_ctx", "norm_mix_g", "norm_ffn_g", "final_norm_g", "w_ada",
        "b_ada", "w_in", "w_out", "conv_a_w", "conv_b_w", "conv_b_b", "ln_b_g", "ln_b_b", "lb_logits",
        "gnorm_c_g", "w_router", "b_router", "w_gate", "w_up", "w_down"]
_OUTS = [(1, CTX, D), (1, LAT, D), (1, 1, 2, HEADS, P, P)]


def kernel(**inputs):
    import numpy as _np
    import concourse.bacc as _bacc
    from concourse.bass_utils import run_bass_kernel_spmd as _run

    nc = _bacc.Bacc("TRN2", target_bir_lowering=False, num_devices=1)
    arrays, args = {}, []
    for name in _INS:
        a = _np.ascontiguousarray(inputs[name])
        arrays[f"in_{name}"] = a
        args.append(nc.dram_tensor(f"in_{name}", a.shape, mybir.dt.from_np(a.dtype), kind="ExternalInput").ap())
    for i, shape in enumerate(_OUTS):
        args.append(nc.dram_tensor(f"out_{i}", shape, F32, kind="ExternalOutput").ap())
    build(nc, *args)
    r = _run(nc, [arrays], core_ids=[0])
    return tuple(r.results[0][f"out_{i}"] for i in range(len(_OUTS)))
```
